# Optimizing a Trainium2 kernel written in Bass

```python
import jax, jax.numpy as jnp
from jax import lax
import numpy as np

D_MODEL = 1024
BATCH = 1
SEQ = 128
DEPTH = 1
DEC_BATCH = 1
DEC_SEQ = 512
PAST_LEN = 128

GRID_W = 64
CONV_DIM = 512
CONV_WIDTH = 31
NA_HEADS = 8
HEAD_DIM = 64
NA_DIM = NA_HEADS * HEAD_DIM
NA_KH = 8
NA_KW = 16
NA_QB = 16
NA_KB = NA_QB + NA_KW
NA_NCB = GRID_W // NA_QB
FNET_GROUPS = 4
FNET_DIM = 512
FNET_GROUP_DIM = FNET_DIM // FNET_GROUPS
N_BRANCHES = 3
IN_DIM = 2 * CONV_DIM + 3 * NA_DIM + FNET_DIM + N_BRANCHES * D_MODEL
SPLITS = (2 * CONV_DIM, 2 * CONV_DIM + NA_DIM, 2 * CONV_DIM + 2 * NA_DIM, 2 * CONV_DIM + 3 * NA_DIM, 2 * CONV_DIM + 3 * NA_DIM + FNET_DIM)
N_EXPERTS = 16
CAPACITY_FACTOR = 2
D_EXPERT = 1024
CTX_Q_BLOCK = 128
EPS = 1e-6
NEG_INF = -1e30

kernel_name = 'hybrid_diffusion_trunk_step'

def _rms_norm(x, g):
    xf = x.astype(jnp.float32)
    y = xf * lax.rsqrt(jnp.mean(xf * xf, axis=-1, keepdims=True) + EPS)
    return (y * g.astype(jnp.float32)).astype(x.dtype)

def _layer_norm(x, g, b):
    xf = x.astype(jnp.float32)
    mu = jnp.mean(xf, axis=-1, keepdims=True)
    var = jnp.mean(jnp.square(xf - mu), axis=-1, keepdims=True)
    y = (xf - mu) * lax.rsqrt(var + EPS)
    return (y * g.astype(jnp.float32) + b.astype(jnp.float32)).astype(x.dtype)

def _conv_module(u2, p):
    a, b = jnp.split(u2, 2, axis=-1)
    u = a * jax.nn.sigmoid(b)
    y = lax.conv_general_dilated(u, p['conv_w'][:, None, :].astype(u.dtype), window_strides=(1,),
                                 padding=((CONV_WIDTH // 2, CONV_WIDTH // 2),),
                                 dimension_numbers=('NWC', 'WIO', 'NWC'), feature_group_count=CONV_DIM)
    y = jax.nn.silu(_layer_norm(y + p['conv_b'], p['conv_ln_g'], p['conv_ln_b']))
    return y @ p['w_conv_out']

def _fourier(f, w_f):
    B, L, _ = f.shape
    fg = f.reshape(B, L, FNET_GROUPS, FNET_GROUP_DIM).astype(jnp.float32)
    z = jnp.fft.fft2(fg, axes=(1, 3), norm='ortho').real.astype(f.dtype)
    return z.reshape(B, L, FNET_DIM) @ w_f

def _context_attention(q, k, v):
    B, L, H, Dh = q.shape
    nb = L // CTX_Q_BLOCK
    scale = HEAD_DIM ** -0.5
    qb = q.reshape(B, nb, CTX_Q_BLOCK, H, Dh).transpose(1, 0, 2, 3, 4)

    def block(qi):
        s = jnp.einsum('bqhd,blhd->bhql', qi, k).astype(jnp.float32) * scale
        pr = jax.nn.softmax(s, axis=-1).astype(v.dtype)
        return jnp.einsum('bhql,blhd->bqhd', pr, v)

    o = lax.map(block, qb)
    return o.transpose(1, 0, 2, 3, 4).reshape(B, L, H * Dh)

def _neighborhood_attention(q, k, v, kc, vc, rpb):
    B, S, H, Dh = q.shape
    R = S // GRID_W
    kh = min(NA_KH, R)
    scale = HEAD_DIM ** -0.5
    rows = jnp.arange(R)
    row_start = jnp.clip(rows - kh // 2, 0, R - kh)
    row_idx = row_start[:, None] + jnp.arange(kh)
    cols = jnp.arange(GRID_W).reshape(NA_NCB, NA_QB)
    col_start = jnp.clip(cols - NA_KW // 2, 0, GRID_W - NA_KW)
    kb = jnp.clip(jnp.arange(NA_NCB) * NA_QB - NA_KW // 2, 0, GRID_W - NA_KB)
    col_idx = kb[:, None] + jnp.arange(NA_KB)
    kg = k.reshape(B, R, GRID_W, H, Dh)
    vg = v.reshape(B, R, GRID_W, H, Dh)
    gi_r = row_idx[:, :, None, None]
    gi_c = col_idx[None, None, :, :]
    k_strip = kg[:, gi_r, gi_c]
    v_strip = vg[:, gi_r, gi_c]
    qg = q.reshape(B, R, NA_NCB, NA_QB, H, Dh)
    s_win = jnp.einsum('brnqhd,brknjhd->bhrnqkj', qg, k_strip).astype(jnp.float32) * scale
    key_col = col_idx[:, None, :]
    cs = col_start[:, :, None]
    valid = (key_col >= cs) & (key_col < cs + NA_KW)
    dr = row_idx - rows[:, None] + (NA_KH - 1)
    dc = jnp.clip(key_col - cols[:, :, None] + (NA_KW - 1), 0, 2 * NA_KW - 2)
    bias = rpb[:, dr[:, None, None, :, None], dc[None, :, :, None, :]]
    s_win = jnp.where(valid[None, None, None, :, :, None, :], s_win + bias.astype(jnp.float32)[None], NEG_INF)
    s_ctx = jnp.einsum('brnqhd,blhd->bhrnql', qg, kc).astype(jnp.float32) * scale
    nw = kh * NA_KB
    s = jnp.concatenate([s_win.reshape(B, H, R, NA_NCB, NA_QB, nw), s_ctx], axis=-1)
    pr = jax.nn.softmax(s, axis=-1).astype(v.dtype)
    p_win = pr[..., :nw].reshape(B, H, R, NA_NCB, NA_QB, kh, NA_KB)
    p_ctx = pr[..., nw:]
    o = jnp.einsum('bhrnqkj,brknjhd->brnqhd', p_win, v_strip) + jnp.einsum('bhrnql,blhd->brnqhd', p_ctx, vc)
    return o.reshape(B, S, H * Dh)

def _mixing(h, p, kv_ctx):
    B, L, _ = h.shape
    u2, q, k, v, f, g = jnp.split(h @ p['w_in'], SPLITS, axis=-1)
    q = q.reshape(B, L, NA_HEADS, HEAD_DIM)
    k = k.reshape(B, L, NA_HEADS, HEAD_DIM)
    v = v.reshape(B, L, NA_HEADS, HEAD_DIM)
    conv_out = _conv_module(u2, p)
    if kv_ctx is None:
        attn = _context_attention(q, k, v)
    else:
        attn = _neighborhood_attention(q, k, v, kv_ctx[0], kv_ctx[1], p['rpb'])
    attn_out = attn @ p['w_na_out']
    fnet_out = _fourier(f, p['w_fnet'])
    gates = jax.nn.sigmoid(g).reshape(B, L, N_BRANCHES, D_MODEL)
    merged = gates[:, :, 0] * conv_out + gates[:, :, 1] * attn_out + gates[:, :, 2] * fnet_out
    return merged @ p['w_out'], k, v

def _expert_choice_ffn(h, p):
    B, S, D = h.shape
    cap = CAPACITY_FACTOR * S // N_EXPERTS
    logits = (h @ p['w_router']).astype(jnp.float32) + p['b_router'].astype(jnp.float32)
    aff = jax.nn.softmax(logits, axis=-1)
    gate, idx = lax.top_k(aff.transpose(0, 2, 1), cap)
    xs = jax.vmap(lambda hb, ib: hb[ib])(h, idx)
    gg = jnp.einsum('becd,edf->becf', xs, p['w_e_gate'])
    uu = jnp.einsum('becd,edf->becf', xs, p['w_e_up'])
    y = jnp.einsum('becf,efd->becd', jax.nn.silu(gg) * uu, p['w_e_down']) * gate[..., None].astype(h.dtype)
    return jax.vmap(lambda yb, ib: jnp.zeros((S, D), yb.dtype).at[ib.reshape(-1)].add(yb.reshape(-1, D)))(y, idx)

def _layer(x, cvec, p, kv_ctx):
    mod = jax.nn.silu(cvec) @ p['w_ada'] + p['b_ada']
    sh1, sc1, g1, sh2, sc2, g2 = [m[:, None, :] for m in jnp.split(mod, 6, axis=-1)]
    h = _rms_norm(x, p['norm1_g']) * (1 + sc1) + sh1
    mix, k, v = _mixing(h, p, kv_ctx)
    x = x + g1 * mix
    h2 = _rms_norm(x, p['norm2_g']) * (1 + sc2) + sh2
    x = x + g2 * _expert_choice_ffn(h2, p)
    return x, k, v

def _normal(k, shape, scale):
    return jax.random.normal(k, shape, jnp.float32) * scale

def setup_inputs(seed: int = 0) -> dict:
    key = jax.random.key(seed)
    ks = jax.random.split(key, 26)
    D = D_MODEL
    return {
        'x_prompt': _normal(ks[0], (BATCH, SEQ, D), 1.0),
        'x_sample': _normal(ks[1], (DEC_BATCH, DEC_SEQ, D), 1.0),
        'cache_k': _normal(ks[2], (DEC_BATCH, DEPTH, PAST_LEN, NA_HEADS, HEAD_DIM), 1.0),
        'cache_v': _normal(ks[3], (DEC_BATCH, DEPTH, PAST_LEN, NA_HEADS, HEAD_DIM), 1.0),
        'c': _normal(ks[4], (DEC_BATCH, D), 1.0),
        'c_ctx': _normal(ks[5], (D,), 1.0),
        'w_ada': _normal(ks[6], (DEPTH, D, 6 * D), 0.5 * D ** -0.5),
        'b_ada': _normal(ks[7], (DEPTH, 6 * D), 0.02),
        'norm1_g': 1.0 + _normal(ks[8], (DEPTH, D), 0.05),
        'w_in': _normal(ks[9], (DEPTH, D, IN_DIM), D ** -0.5),
        'conv_w': _normal(ks[10], (DEPTH, CONV_WIDTH, CONV_DIM), CONV_WIDTH ** -0.5),
        'conv_b': _normal(ks[11], (DEPTH, CONV_DIM), 0.02),
        'conv_ln_g': 1.0 + _normal(ks[12], (DEPTH, CONV_DIM), 0.05),
        'conv_ln_b': _normal(ks[13], (DEPTH, CONV_DIM), 0.02),
        'w_conv_out': _normal(ks[14], (DEPTH, CONV_DIM, D), CONV_DIM ** -0.5),
        'rpb': _normal(ks[15], (DEPTH, NA_HEADS, 2 * NA_KH - 1, 2 * NA_KW - 1), 0.1),
        'w_na_out': _normal(ks[16], (DEPTH, NA_DIM, D), NA_DIM ** -0.5),
        'w_fnet': _normal(ks[17], (DEPTH, FNET_DIM, D), FNET_DIM ** -0.5),
        'w_out': _normal(ks[18], (DEPTH, D, D), D ** -0.5),
        'norm2_g': 1.0 + _normal(ks[19], (DEPTH, D), 0.05),
        'w_router': _normal(ks[20], (DEPTH, D, N_EXPERTS), D ** -0.5),
        'b_router': _normal(ks[21], (DEPTH, N_EXPERTS), 0.01),
        'w_e_gate': _normal(ks[22], (DEPTH, N_EXPERTS, D, D_EXPERT), D ** -0.5),
        'w_e_up': _normal(ks[23], (DEPTH, N_EXPERTS, D, D_EXPERT), D ** -0.5),
        'w_e_down': _normal(ks[24], (DEPTH, N_EXPERTS, D_EXPERT, D), D_EXPERT ** -0.5),
        'final_norm_g': 1.0 + _normal(ks[25], (D,), 0.05),
    }

def reference(x_prompt, x_sample, cache_k, cache_v, c, c_ctx, w_ada, b_ada, norm1_g, w_in, conv_w, conv_b,
              conv_ln_g, conv_ln_b, w_conv_out, rpb, w_na_out, w_fnet, w_out, norm2_g, w_router, b_router,
              w_e_gate, w_e_up, w_e_down, final_norm_g):
    params = []
    for l in range(DEPTH):
        params.append({
            'w_ada': w_ada[l], 'b_ada': b_ada[l], 'norm1_g': norm1_g[l], 'w_in': w_in[l],
            'conv_w': conv_w[l], 'conv_b': conv_b[l], 'conv_ln_g': conv_ln_g[l], 'conv_ln_b': conv_ln_b[l],
            'w_conv_out': w_conv_out[l], 'rpb': rpb[l], 'w_na_out': w_na_out[l], 'w_fnet': w_fnet[l],
            'w_out': w_out[l], 'norm2_g': norm2_g[l], 'w_router': w_router[l], 'b_router': b_router[l],
            'w_e_gate': w_e_gate[l], 'w_e_up': w_e_up[l], 'w_e_down': w_e_down[l],
        })

    xp = x_prompt
    c_ctx_b = c_ctx[None, :]
    ks_new, vs_new = [], []
    for l in range(DEPTH):
        xp, k_l, v_l = _layer(xp, c_ctx_b, params[l], None)
        ks_new.append(k_l)
        vs_new.append(v_l)
    y_prompt = _rms_norm(xp, final_norm_g)
    new_k = jnp.stack(ks_new, axis=1)
    new_v = jnp.stack(vs_new, axis=1)

    xs = x_sample
    for l in range(DEPTH):
        xs, _, _ = _layer(xs, c, params[l], (cache_k[:, l], cache_v[:, l]))
    y_sample = _rms_norm(xs, final_norm_g)

    return (y_prompt, y_sample, new_k, new_v)


_drawn_inputs = setup_inputs


def setup_inputs(seed=0):
    import zlib

    import numpy as np

    out = dict(_drawn_inputs(seed))
    spreads = {}
    factors = {'cache_k': 5.701,
     'cache_v': 4.771,
     'conv_b': 8.0,
     'conv_ln_g': 8.0,
     'conv_ln_b': 8.0,
     'rpb': 64.0,
     'norm2_g': 5.252,
     'b_router': 8.0}
    for name, (base, spread) in spreads.items():
        noise = np.random.default_rng([zlib.crc32(name.encode()), seed]).standard_normal(out[name].shape)
        drawn = base * np.exp(spread * noise) if base else spread * noise
        out[name] = __import__('jax').numpy.asarray(drawn.astype(out[name].dtype))
    for name, factor in factors.items():
        out[name] = (out[name] * factor).astype(out[name].dtype)
    return out
```

```python
from contextlib import ExitStack

import numpy as np
import concourse.bass as bass
from concourse import mybir

F32 = mybir.dt.float32
F32R = mybir.dt.float32r
U32 = mybir.dt.uint32
ALU = mybir.AluOpType
ACT = mybir.ActivationFunctionType
AX = mybir.AxisListType.X

P = 128
D = 1024
DC = D // P
NP, NS = 128, 512
T = NP + NS
TT = T // P
H, DH = 8, 64
GW = 64
ROWS = NS // GW
CW = 31
PADW = CW // 2
CB = 4
E_N = 16
FE = 1024
CAP_S, CAP_P = 2 * NS // E_N, 2 * NP // E_N
M_E = CAP_S + CAP_P
EPS = 1e-6
UN = 2048
SCALE = DH ** -0.5
BW = 48
RPL = 32 + 120 * BW
U_P, U_S = PADW, PADW + NP + PADW
U_N = U_S + NS + PADW
Y_S = U_S - PADW
Y_N = Y_S + NS

UNITS = [("ada", i) for i in range(8)]
for _i in range(4):
    UNITS += [("in", _i)] + [("ada", 8 + 4 * _i + _j) for _j in range(4)]
UNITS += [("in", 10), ("in", 11), ("dft", 0), ("dft", 1)]
UNITS += [("in", i) for i in range(4, 10)]
UNITS += [("in", i) for i in range(20, 24)] + [("fnet", 0), ("fnet", 1)]
UNITS += [("in", i) for i in range(16, 20)] + [("na", 0), ("na", 1)]
UNITS += [("in", i) for i in range(12, 16)] + [("conv", 0), ("conv", 1)]
UNITS += [("out", i) for i in range(4)]
U_OF = {u: n for n, u in enumerate(UNITS)}
N_U = len(UNITS)


def lo_count(engine, n):
    return sum((UNITS[i][0] == "ada") == (engine == "dve") for i in range(n))


JOBS = [("xT", i) for i in range(DC)]
JOBS += [("u2", i) for i in range(8)]
JOBS += [("f", i) for i in range(4)]
JOBS += [("uv", 0, t) for t in range(TT)]
for _g in range(4):
    if _g < 3:
        JOBS += [("uv", _g + 1, t) for t in range(TT)]
    JOBS += [("z", _g)]
JOBS += [("q", i) for i in range(4)] + [("k", i) for i in range(4)]
JOBS += [("v", u, t) for u in range(2) for t in range(TT)]
JOBS += [("g2", i) for i in range(DC)] + [("fnet", i) for i in range(DC)]
JOBS += [("g1", i) for i in range(DC)] + [("na", i) for i in range(DC)]
JOBS += [("g0", i) for i in range(DC)] + [("conv", i) for i in range(DC)]
TILE_ORDER = [1, 2, 3, 4, 0]
JOBS += [("out", u, t) for u in range(4) for t in TILE_ORDER]
IN_JOBS = [("u2", 0), ("q", 4), ("k", 6), ("v", 8), ("f", 10), ("g0", 12), ("g1", 16), ("g2", 20)]
J_OF = {j: n for n, j in enumerate(JOBS)}
BY_DVE = ("f", "uv", "fnet", "na", "conv", "out")


def freed(n):
    dve = JOBS[n][0] in BY_DVE
    return dve, sum((JOBS[i][0] in BY_DVE) == dve for i in range(n + 1))


ITEMS = [(-1, h) for h in range(H)] + [(n, h) for n in range(4) for h in range(H)]
KB = [0, 8, 24, 32]
VARIANT = [0, 1, 1, 2]
U_OFF = [16, 8, 8, 0]


def trunk(nc, a, outs, consts, scratch):
    y_prompt, y_sample, new_k, new_v = outs
    mods_d, rpb_d, v_d, h2_d, acc_d = scratch

    w_in = a["w_in"][0].rearrange("(c p) n -> p c n", p=P)
    w_ada = a["w_ada"][0].rearrange("(c p) n -> p c n", p=P)
    w_br = {"fnet": a["w_fnet"][0], "na": a["w_na_out"][0], "conv": a["w_conv_out"][0]}
    w_out = a["w_out"][0].rearrange("(c p) n -> p c n", p=P)

    def unit_src(u):
        kind, i = UNITS[u]
        if kind == "ada":
            return w_ada[:, :, i * 256:(i + 1) * 256]
        if kind == "in":
            return w_in[:, :, i * 256:(i + 1) * 256]
        if kind == "dft":
            return consts["dft_l"][i]
        if kind == "out":
            return w_out[:, :, i * 256:(i + 1) * 256]
        return w_br[kind].rearrange("(c p) n -> p c n", p=P)[:, :, i * 512:(i + 1) * 512]

    def unit_view(x, u):
        c = CB if UNITS[u][0] in ("fnet", "na", "conv", "dft") else DC
        return x.rearrange("p (c n) -> p c n", c=c)

    with ExitStack() as ctx:
        def sem(name):
            return ctx.enter_context(nc.semaphore(name))

        def place(stack, name, shape, dt=F32):
            return stack.enter_context(nc.sbuf_tensor(name, shape, dt))

        ident = place(ctx, "ident", [P, P])
        ones = place(ctx, "ones", [P, P])
        gtab_h = place(ctx, "gtab_h", [P, 384], F32R)
        gtab_l = place(ctx, "gtab_l", [P, 384], F32R)
        mask = place(ctx, "mask", [P, 3, 32])
        sel4 = place(ctx, "sel4", [4, 2])
        cwT = place(ctx, "cwT", [P, CB, CW])
        colsT = place(ctx, "colsT", [P, 20])
        modcol = place(ctx, "modcol", [P, 16, 2])
        A1 = place(ctx, "A1", [P, DC, 2])
        stat = place(ctx, "stat", [P, 52])
        half = place(ctx, "half", [P, 8])
        hlnb = place(ctx, "hlnb", [P, 8])
        idxT = place(ctx, "idxT", [M_E, E_N], U32)
        gateT = place(ctx, "gateT", [M_E, E_N])
        idx_g = place(ctx, "idx_g", [M_E, 1], U32)
        idx_s = place(ctx, "idx_s", [M_E, 1], U32)

        with ExitStack() as p1:
            wring = place(p1, "wring", [P, 2, UN])
            hring = place(p1, "hring", [P, 2, UN], F32R)
            lring = place(p1, "lring", [P, 2, UN], F32R)
            hTh = place(p1, "hTh", [P, DC, T], F32R)
            hTl = place(p1, "hTl", [P, DC, T], F32R)
            with ExitStack() as t0:
                tmp5 = place(t0, "tmp5", [P, 4, T])
                c4 = place(t0, "c4", [P, DC, P], F32R)
            with ExitStack() as t1:
                vw = place(t1, "vw", [P, 2, 2, 512])
                bm = place(t1, "bm", [P, 2, 8, 32])
                sp = place(t1, "sp", [P, 2, 384])
                pT = place(t1, "pT", [P, 2, 384])
            bh = place(p1, "bh", [P, CB, T], F32R)
            bl = place(p1, "bl", [P, CB, T], F32R)
            with ExitStack() as t2:
                uvh = place(t2, "uvh", [P, 2, TT, 256], F32R)
                uvl = place(t2, "uvl", [P, 2, TT, 256], F32R)
            xg_f = place(p1, "xg_f", [P, TT * D])
            fa = place(p1, "fa", [P, 17648])
        X = xg_f[:, :].rearrange("p (t d) -> p t d", t=TT)
        G = xg_f[:, :].rearrange("p (b t) -> p b t", b=DC)
        Vs = xg_f[:, 0:2048].rearrange("p (t d) -> p t d", t=4)
        Z = fa[:, 0:2560].rearrange("p (c t) -> p c t", c=CB)
        Q = fa[:, 2560:5120].rearrange("p (c t) -> p c t", c=CB)
        K = fa[:, 5120:7680].rearrange("p (c t) -> p c t", c=CB)
        Bt = fa[:, 7680:10752].rearrange("p (h r u) -> p h r u", h=H, r=8)
        M = fa[:, 5120:10240].rearrange("p (b t) -> p b t", b=DC)
        U = fa[:, 10752:10752 + CB * U_N].rearrange("p (c t) -> p c t", c=CB)
        Y = fa[:, 13492:13492 + CB * Y_N].rearrange("p (c t) -> p c t", c=CB)
        SM = 16112
        kcT = fa[:, SM:SM + 512].rearrange("p (c t) -> p c t", c=CB)
        vc = fa[:, SM + 512:SM + 1024]
        vp = fa[:, SM + 1024:SM + 1536]
        rows4 = fa[0:4, 0:512].rearrange("p (b n) -> p b n", b=2)
        modrow = fa[0:2, 512:1024].rearrange("p (b n) -> p b n", b=2)
        modall = xg_f[0:2, 0:4 * D]
        brow = fa[0:1, 2560:2560 + 6144]
        c2 = fa[0:2, 13492:13492 + D]
        rows20 = fa[0:20, 14516:14516 + P]
        cwr = fa[0:CW, 14644:14644 + 512]
        kraw = fa[:, 15156:15156 + 512]
        graw = fa[:, 1024:1408]
        cs = fa[:, 1408:1424]
        cs2 = fa[:, 1424:1440]
        cs3 = fa[:, 1440:1456]
        rpad = fa[0:120, 1536:1536 + BW]
        Yc = fa[:, 10752:13312].rearrange("p (c t) -> p c t", c=CB)
        Yq = fa[:, 13492:16052].rearrange("p (c t) -> p c t", c=CB)
        diag = fa[:, 0:640]
        g1bc = fa[:, 0:2048].rearrange("p (g d) -> p g d", g=2)
        A2bc = fa[:, 10752:12800].rearrange("p (g d) -> p g d", g=2)
        sh2bc = fa[:, 12800:14848].rearrange("p (g d) -> p g d", g=2)
        n2bc = fa[:, 14848:15872]
        otmp = fa[:, 2560:3072].rearrange("p (b n) -> p b n", b=2)
        h2t = fa[:, 5120:7168].rearrange("p (b d) -> p b d", b=2)
        h2T = fa[:, 7168:9216].rearrange("p (b c t) -> p b c t", b=2, c=DC)
        junk = fa[:, 9216:10240]
        wr = fa[:, 3072:3200].rearrange("p (c e) -> p c e", c=DC)
        br = fa[0:1, 3200:3216]
        lgs = fa[:, 3296:3376].rearrange("p (t e) -> p t e", t=TT)
        aff = fa[:, 3216:3296].rearrange("p (t e) -> p t e", t=TT)
        affT = fa[0:E_N, SM:SM + T]
        vals = fa[0:E_N, SM + 640:SM + 720]
        idxf = fa[0:E_N, SM + 720:SM + 800]
        idxu = fa[0:E_N, SM + 800:SM + 880].bitcast(U32)

        with ExitStack() as p2:
            w2 = place(p2, "w2", [P, 6, UN])
            h2r = place(p2, "h2r", [P, 3, UN], F32R)
            l2r = place(p2, "l2r", [P, 3, UN], F32R)
            place(p2, "gap", [P, 8192])
            xe = place(p2, "xe", [M_E, D])
            xTh = place(p2, "xTh", [P, DC, M_E], F32R)
            xTl = place(p2, "xTl", [P, DC, M_E], F32R)
            sg = place(p2, "sg", [M_E, D])
            hTh2 = place(p2, "hTh2", [P, DC, M_E], F32R)
            hTl2 = place(p2, "hTl2", [P, DC, M_E], F32R)
            ye = place(p2, "ye", [M_E, D])
            g2r = place(p2, "g2r", [M_E, D])
        fin = xg_f[:, :].rearrange("p (t d) -> p t d", t=TT)
        fgbc = fa[:, 10752:11776]

        bank = [ctx.enter_context(nc.psum_tensor(f"bank{i}", [P, 512], F32)) for i in range(8)]
        def job_bank(n):
            return bank[n % 2][:, :], bank[2 + n % 2][:, 0:P]

        s_cst = sem("s_cst"); s_x = sem("s_x"); s_cast = sem("s_cast")
        s_rpad = sem("s_rpad"); s_rpb1 = sem("s_rpb1"); s_rpb2 = sem("s_rpb2"); s_bt = sem("s_bt")
        s_w = [sem("s_w0"), sem("s_w1")]
        s_hi = sem("s_hi"); s_lov = sem("s_lov"); s_lop = sem("s_lop")
        s_job = sem("s_job"); s_ja = sem("s_ja"); s_jd = sem("s_jd")
        s_turn = sem("s_turn"); s_turned = sem("s_turned"); s_c4 = sem("s_c4")
        s_ada = sem("s_ada"); s_rows4 = sem("s_rows4"); s_mrow = sem("s_mrow"); s_modrow = sem("s_modrow")
        s_mcol = sem("s_mcol"); s_modcol = sem("s_modcol"); s_modst = sem("s_modst")
        s_ssq = sem("s_ssq"); s_rstd = sem("s_rstd"); s_xhat = sem("s_xhat")
        s_a1 = sem("s_a1"); s_hh = sem("s_hh"); s_h = sem("s_h")
        s_tb = sem("s_tb"); s_u = sem("s_u"); s_fh = sem("s_fh"); s_uvh = sem("s_uvh")
        s_cv = sem("s_cv"); s_vst = sem("s_vst"); s_vw = [sem("s_vwa"), sem("s_vwb")]
        s_kt = sem("s_kt"); s_ko = sem("s_ko"); s_out = sem("s_out")
        s_sc = sem("s_sc"); s_bm = sem("s_bm"); s_ev = sem("s_ev"); s_mx = sem("s_mx"); s_ex = sem("s_ex")
        s_pn = sem("s_pn"); s_pt = sem("s_pt"); s_pte = sem("s_pte"); s_pv = sem("s_pv"); s_at = sem("s_at")
        s_bh = sem("s_bh"); s_bl = sem("s_bl")
        s_ln = sem("s_ln"); s_lnd = sem("s_lnd"); s_lnc = sem("s_lnc"); s_lns = sem("s_lns"); s_lnr = sem("s_lnr"); s_yc = sem("s_yc"); s_ysq = sem("s_ysq")
        s_yr = sem("s_yr"); s_yt = sem("s_yt"); s_yz = sem("s_yz")
        s_bc = sem("s_bc"); s_x2 = sem("s_x2"); s_xr = sem("s_xr")
        s_q2 = sem("s_q2"); s_r2 = sem("s_r2"); s_h2 = sem("s_h2"); s_hst = [sem("s_hsta"), sem("s_hstb")]; s_xst = sem("s_xst")
        s_t2 = sem("s_t2"); s_t2e = sem("s_t2e"); s_lg = sem("s_lg"); s_lgc = sem("s_lgc"); s_mx2 = sem("s_mx2"); s_ex2 = sem("s_ex2")
        s_aff = sem("s_aff"); s_affp = sem("s_affp"); s_idx = sem("s_idx"); s_idxp = sem("s_idxp")
        s_route = sem("s_route"); s_va = sem("s_va"); s_gm = sem("s_gm"); s_a2 = sem("s_a2"); s_xp = sem("s_xp"); s_u0 = sem("s_u0"); s_aa = sem("s_aa"); s_pa = sem("s_pa")
        e_w = [sem(f"e_w{i}") for i in range(6)]
        e_hi = sem("e_hi"); e_lo = sem("e_lo"); e_unit = sem("e_unit")
        e_col = sem("e_col"); e_x = sem("e_x"); e_xt = sem("e_xt"); e_xh = sem("e_xh"); e_xl = sem("e_xl")
        e_sg = sem("e_sg"); e_h = sem("e_h"); e_ht = sem("e_ht"); e_hh = sem("e_hh"); e_hl = sem("e_hl")
        e_y = sem("e_y"); e_cs = sem("e_cs"); e_add = sem("e_add"); s_g2 = sem("s_g2")
        s_fin = sem("s_fin"); s_fq = sem("s_fq"); s_fr = sem("s_fr"); s_fy = sem("s_fy")

        N_CST = 14

        def at(e):
            return slice(e, e + 1) if isinstance(e, int) else bass.ds(e, 1)

        block = ctx.enter_context(nc.Block())

        def by_block(x):
            return x.rearrange("p (n r i) -> p r n i", n=4, r=ROWS)

        def unit_used(eng, u):
            kind, i = UNITS[u]
            if kind == "ada":
                eng.wait_ge(s_ada, i + 1)
                return
            last = {"in": ("in", i), "dft": ("z", 3), "out": ("out", i, 0)}.get(kind, (kind, 4 * i + 3))
            if kind == "in":
                name, first = [(n, f) for n, f in IN_JOBS if f <= i][-1]
                last = (name, i - first, TT - 1) if name == "v" else (name, 2 * (i - first) + 1)
            eng.wait_ge(s_job, J_OF[last] + 1)

        def lo_ready(eng, u):
            if UNITS[u][0] == "ada":
                eng.wait_ge(s_lov, lo_count("dve", u + 1))
            else:
                eng.wait_ge(s_lop, lo_count("pool", u + 1))

        @block.sync
        def _(sp):
            for dst, src in ((ident[:, :], consts["ident"]), (ones[:, :], consts["ones"]), (mask[:, :, :], consts["mask"]),
                             (sel4[:, :], consts["sel4"]), (graw, consts["dft_g"]), (cwr, a["conv_w"][0]),
                             (c2[0:1, :], a["c_ctx"].rearrange("(o d) -> o d", o=1)), (c2[1:2, :], a["c"]),
                             (brow, a["b_ada"]), (kraw, a["cache_k"][0, 0].rearrange("l h d -> l (h d)"))):
                sp.dma_start(dst, src).then_inc(s_cst, 16)
            for r0, src in ((0, a["norm1_g"][0]), (8, a["conv_b"][0]), (12, a["conv_ln_g"][0]), (16, a["conv_ln_b"][0])):
                n = src.shape[0] // P
                sp.dma_start(rows20[r0:r0 + n, :], src.rearrange("(c p) -> c p", p=P)).then_inc(s_cst, 16)

            def unit(u):
                if u >= 2:
                    lo_ready(sp, u - 2)
                sp.dma_start(unit_view(wring[:, u % 2, :], u), unit_src(u)).then_inc(s_w[u % 2], 16)

            unit(0)
            sp.dma_start(X[:, 0, :], a["x_prompt"][0]).then_inc(s_x, 16)
            for t in range(4):
                sp.dma_start(X[:, 1 + t, :], a["x_sample"][0, t * P:(t + 1) * P, :]).then_inc(s_x, 16)
            sp.dma_start(vc, a["cache_v"][0, 0].rearrange("l h d -> l (h d)")).then_inc(s_x, 16)
            for u in range(1, N_U):
                unit(u)
            unit_used(sp, N_U - 1)

            def expert(e):
                for k in range(12):
                    name = ("w_e_gate", "w_e_up", "w_e_down")[k // 4]
                    q = k % 4
                    src = a[name][0, at(e), 256 * q:256 * q + 256, :].rearrange("o (c p) n -> p (o c) n", p=P)
                    if isinstance(e, int) and e == 0:
                        if k >= 6:
                            sp.wait_ge(e_lo, k - 5)
                    else:
                        sp.wait_ge(e_lo, 12 * e + (k - 5))
                    sp.dma_start(w2[:, k % 6, :].rearrange("p (c n) -> p c n", c=2), src).then_inc(e_w[k % 6], 16)

            expert(0)
            with sp.Fori(1, E_N) as e:
                expert(e)

        @block.gpsimd
        def _(gp):
            gp.memset(rpad, 0.0).then_inc(s_rpad, 1)
            gp.memset(half[:, :], -0.5).then_inc(s_pa, 1)
            gp.wait_ge(s_rpad, 1)
            gp.dma_start(rpb_d[:, 0:32], rpad[0:16, 0:32]).then_inc(s_rpb1, 16)
            gp.wait_ge(s_rpb1, 16)
            gp.dma_start(rpad[:, 0:31], a["rpb"][0].rearrange("h a b -> (h a) b")).then_inc(s_rpb1, 16)
            gp.wait_ge(s_rpb1, 32)
            gp.dma_start(bass.AP(rpb_d.tensor, 16, [[BW, 120], [RPL + 1, 16], [1, BW]]),
                         rpad.unsqueeze(1).to_broadcast([120, 16, BW])).then_inc(s_rpb2, 16)
            gp.wait_ge(s_ssq, TT)
            gp.tensor_scalar(stat[:, 5:10], stat[:, 0:5], 1.0 / D, EPS, ALU.mult, ALU.add).then_inc(s_pa, 1)
            gp.wait_ge(s_pa, 2)
            gp.tensor_tensor(stat[:, 10:15], stat[:, 5:10], half[:, 0:5], ALU.pow).then_inc(s_rstd, 1)

            def lo(u):
                gp.wait_ge(s_hi, u + 1)
                gp.tensor_tensor(lring[:, u % 2, :], wring[:, u % 2, :], hring[:, u % 2, :].bitcast(F32),
                                 ALU.subtract).then_inc(s_lop, 1)

            todo = [u for u in range(N_U) if UNITS[u][0] != "ada"]
            at_attention = todo.index(U_OF[("in", 20)])
            for u in todo[:4]:
                lo(u)
            gp.wait_ge(s_rpb2, 16)
            gp.wait_ge(s_modst, 16)
            for r in range(8):
                src = bass.AP(rpb_d.tensor, 16 + (7 - r) * BW - 1, [[RPL, 16], [15 * BW, H], [1, 8 * BW]])
                gp.dma_start(Bt[16 * r:16 * r + 16].rearrange("p h r u -> p h (r u)"), src).then_inc(s_bt, 16)
            for u in todo[4:at_attention]:
                lo(u)
            rest = todo[at_attention:]
            gp.wait_ge(s_bt, 16 * 8)
            n = 0
            for it, (blk, h) in enumerate(ITEMS):
                if it % 8 == 0 and n < 5:
                    lo(rest[n])
                    n += 1
                if blk < 0:
                    continue
                w = it - 8
                if w >= 2:
                    gp.wait_ge(s_ev, it - 1)
                o = U_OFF[blk]
                gp.tensor_tensor(bm[:, w % 2], Bt[:, h, :, o:o + 32],
                                 mask[:, VARIANT[blk], :].unsqueeze(1).to_broadcast([P, 8, 32]), ALU.add).then_inc(s_bm, 1)
            ln = U_OF[("in", 12)] - U_OF[("in", 20)] + 3
            for u in rest[n:ln]:
                lo(u)
            gp.wait_ge(s_lns, 1)
            gp.tensor_tensor(stat[:, 25:30], stat[:, 20:25], half[:, 0:5], ALU.pow).then_inc(s_lnr, 1)
            for u in rest[ln:]:
                lo(u)
            for i, t in enumerate(TILE_ORDER):
                gp.wait_ge(s_q2, i + 1)
                gp.tensor_scalar(stat[:, 5 + t:6 + t], stat[:, t:t + 1], 1.0 / D, EPS, ALU.mult, ALU.add).then_inc(s_pa, 1)
                gp.wait_ge(s_pa, 3 + i)
                gp.tensor_tensor(stat[:, 10 + t:11 + t], stat[:, 5 + t:6 + t], half[:, 0:1], ALU.pow).then_inc(s_r2, 1)
            gp.wait_ge(s_route, 2)
            for st in (s_hst[0], s_hst[1], s_xst):
                gp.wait_ge(st, 16 * {id(s_hst[0]): 3, id(s_hst[1]): 2}.get(id(st), 5))

            def step():
                gp.tensor_tensor(half[0:1, 7:8], half[0:1, 5:6], half[0:1, 6:7], ALU.add)

            def gather(e):
                gp.tensor_copy(idx_g[:, :], idxT[:, at(e)]).then_inc(e_col, 1)
                gp.wait_ge(e_col, e + 1)
                step()
                gp.indirect_dma_start(xe[:, :], None, h2_d, bass.IndirectOffsetOnAxis(idx_g[:, 0:1], 0)).then_inc(e_x, 16)

            gather(0)

            def expert(e, last):
                if not last:
                    gp.wait_ge(e_xt, 2 * e + 2)
                    gather(e + 1)
                if not (isinstance(e, int) and e == 0):
                    gp.wait_ge(e_add, 16 * e)
                gp.tensor_copy(idx_s[:, :], idxT[:, at(e)]).then_inc(e_cs, 1)
                gp.wait_ge(e_cs, e + 1)
                gp.wait_ge(e_y, 2 * e + 2)
                step()
                gp.indirect_dma_start(acc_d, bass.IndirectOffsetOnAxis(idx_s[:, 0:1], 0), ye[:, :], None,
                                      compute_op=ALU.add).then_inc(e_add, 16)

            expert(0, False)
            with gp.Fori(1, E_N - 1) as e:
                expert(e, False)
            expert(E_N - 1, True)
            for t in range(TT):
                gp.wait_ge(s_fq, t + 1)
                gp.tensor_scalar(stat[:, 5 + t:6 + t], stat[:, t:t + 1], 1.0 / D, EPS, ALU.mult, ALU.add).then_inc(s_pa, 1)
                gp.wait_ge(s_pa, 8 + t)
                gp.tensor_tensor(stat[:, 10 + t:11 + t], stat[:, 5 + t:6 + t], half[:, 0:1], ALU.pow).then_inc(s_fr, 1)

        @block.scalar
        def _(act):
            def hi(u):
                act.wait_ge(s_w[u % 2], 16 * (u // 2 + 1))
                if u >= 2:
                    unit_used(act, u - 2)
                act.copy(hring[:, u % 2, :], wring[:, u % 2, :]).then_inc(s_hi, 1)

            def take(n, out_s, out_p, func=ACT.Copy, scale=1.0, signal=None):
                act.wait_ge(s_job, n + 1)
                bs, bp = job_bank(n)
                act.activation(out_s, bs, func, scale=scale)
                return act.activation(out_p, bp, func, scale=scale)

            act.wait_ge(s_x, 16 * 6)
            for t in range(TT):
                act.activation(tmp5[:, 0:2, :].rearrange("p a b -> p (a b)")[:, 0:D], X[:, t, :], ACT.Square,
                               accum_out=stat[:, t:t + 1]).then_inc(s_ssq, 1)
                act.wait_ge(s_ssq, t + 1)
            hi(0); hi(1)
            act.wait_ge(s_turned, 1)
            act.activation(cs2, cs, ACT.Tanh, scale=0.5).then_inc(s_aa, 1)
            act.wait_ge(s_cast, 1)
            act.copy(c4[:, :, 0:2], cs3.rearrange("p (c g) -> p c g", g=2)).then_inc(s_c4, 1)
            act.copy(gtab_h[:, :], graw).then_inc(s_c4, 1)
            for u in range(2, 10):
                hi(u)
            act.wait_ge(s_a1, 1)
            for dc in range(DC):
                n = J_OF[("xT", dc)]
                act.wait_ge(s_job, n + 1)
                if dc >= 4:
                    act.wait_ge(s_h, dc - 3)
                bs, bp = job_bank(n)
                o = tmp5[:, dc % 4, :]
                act.activation(o[:, NP:T], bs, ACT.Identity, bias=modcol[:, dc, 1:2], scale=A1[:, dc, 1:2])
                act.activation(o[:, 0:NP], bp, ACT.Identity, bias=modcol[:, dc, 0:1], scale=A1[:, dc, 0:1]).then_inc(s_ja, 1)
                act.wait_ge(s_ja, dc + 1)
                act.copy(hTh[:, dc, :], o).then_inc(s_hh, 1)
            act.wait_ge(s_u0, 1)
            for i in range(4):
                first = U_OF[("in", i)]
                for b in (2 * i, 2 * i + 1):
                    n = J_OF[("u2", b)]
                    if b < 4:
                        take(n, U[:, b, U_S:U_S + NS], U[:, b, U_P:U_P + NP]).then_inc(s_ja, 1)
                    else:
                        if b >= 6:
                            act.wait_ge(s_u, b - 5)
                        o = tmp5[:, b % 2, :]
                        take(n, o[:, NP:T], o[:, 0:NP], ACT.Tanh, 0.5).then_inc(s_ja, 1)
                for u in range(first + 2, first + 7):
                    hi(u)
            act.wait_ge(s_modrow, 24)
            act.dma_start(mods_d, modall).then_inc(s_modst, 16)
            act.wait_ge(s_u, 4)
            for i in range(4):
                if i == 2:
                    hi(U_OF[("dft", 0)])
                n = J_OF[("f", i)]
                act.wait_ge(s_job, n + 1)
                bs, bp = job_bank(n)
                act.copy(bh[:, i, NP:T], bs)
                act.copy(bh[:, i, 0:NP], bp).then_inc(s_fh, 1)
            hi(U_OF[("dft", 1)])

            def uv_hi(g):
                for t in range(TT):
                    n = J_OF[("uv", g, t)]
                    act.wait_ge(s_job, n + 1)
                    act.copy(uvh[:, g % 2, t, :], bank[n % 2][:, 0:256]).then_inc(s_uvh, 1)

            uv_hi(0)
            for g in range(4):
                if g < 3:
                    uv_hi(g + 1)
                n = J_OF[("z", g)]
                take(n, Z[:, g, NP:T], Z[:, g, 0:NP]).then_inc(s_ja, 1)
            u = U_OF[("in", 4)]
            hi(u); hi(u + 1)
            for kind, dst, base in (("q", Q, u), ("k", K, u + 2)):
                for b in range(4):
                    n = J_OF[(kind, b)]
                    if kind == "q":
                        act.wait_ge(s_job, n + 1)
                        bs, bp = job_bank(n)
                        act.copy(by_block(Q[:, b, NP:T]), bs.rearrange("p (r n i) -> p r n i", r=ROWS, n=4))
                        act.copy(Q[:, b, 0:NP], bp).then_inc(s_ja, 1)
                    else:
                        take(n, dst[:, b, NP:T], dst[:, b, 0:NP]).then_inc(s_ja, 1)
                    if b % 2:
                        hi(base + 2 + b // 2)
            for i in range(2):
                for t in range(TT):
                    n = J_OF[("v", i, t)]
                    act.wait_ge(s_job, n + 1)
                    dst = vp[:, i * 256:(i + 1) * 256] if t == 0 else Vs[:, t - 1, i * 256:(i + 1) * 256]
                    act.copy(dst, bank[n % 2][:, 0:256]).then_inc(s_ja, 1)
                hi(u + 6 + i)
            act.wait_ge(s_kt, 1)
            act.copy(sp[:, :, 0:256], bank[6][:, :].rearrange("p (a b) -> p a b", a=2)).then_inc(s_ko, 1)
            act.wait_ge(s_ko, 1)
            act.dma_start(new_k.rearrange("b l s h d -> (b l s) (h d)").rearrange("s (a b) -> s a b", a=2),
                          sp[:, :, 0:256]).then_inc(s_out, 16)
            act.dma_start(new_v.rearrange("b l s h d -> (b l s) (h d)"), vp).then_inc(s_out, 16)
            act.dma_start(v_d.rearrange("(t p) d -> p t d", p=P), Vs).then_inc(s_vst, 16)
            act.wait_ge(s_vst, 16)
            act.wait_ge(s_out, 32)

            def window_values(blk):
                for c in range(2):
                    src = bass.AP(v_d.tensor, (4 * c * GW + KB[blk]) * 512, [[GW * 512, 4], [512, 32], [1, 512]])
                    act.dma_start(vw[:, blk % 2, c, :], src).then_inc(s_vw[blk % 2], 16)

            window_values(0); window_values(1)
            hi_next = U_OF[("in", 22)]
            for it in range(len(ITEMS) + 2):
                if it < len(ITEMS):
                    blk, h = ITEMS[it]
                    w = it % 2
                    kn = NP if blk < 0 else 384
                    act.wait_ge(s_mx, it + 1)
                    act.activation(sp[:, w, 0:kn], sp[:, w, 0:kn], ACT.Exp, bias=stat[:, 30 + w:31 + w],
                                   accum_out=stat[:, 32 + w:33 + w]).then_inc(s_ex, 1)
                if 1 <= it <= len(ITEMS):
                    j = it - 1
                    blk, h = ITEMS[j]
                    kn = NP if blk < 0 else 384
                    act.wait_ge(s_pt, j + 1)
                    if j >= 2:
                        act.wait_ge(s_pv, j - 1)
                    act.copy(pT[:, j % 2, 0:kn], bank[6][:, 0:kn]).then_inc(s_pte, 1)
                if it >= 2 and ITEMS[it - 2] in ((0, 7), (1, 7)):
                    act.wait_ge(s_pv, it - 1)
                    window_values(ITEMS[it - 2][0] + 2)
                if it % 5 == 4 and it // 5 < DC:
                    b = it // 5
                    n = J_OF[("g2", b)]
                    take(n, G[:, b, NP:T], G[:, b, 0:NP], ACT.Tanh, 0.5).then_inc(s_ja, 1)
                    if b % 2:
                        hi(hi_next); hi_next += 1

            def split_hi(src):
                for c in range(CB):
                    act.copy(bh[:, c, :], src(c)).then_inc(s_bh, 1)

            def gates(kind, first, blocks):
                for b in blocks:
                    n = J_OF[(kind, b)]
                    if first == "fnet":
                        act.wait_ge(s_jd, freed(J_OF[(first, b)])[1])
                    else:
                        act.wait_ge(s_gm, b + 1)
                    take(n, G[:, b, NP:T], G[:, b, 0:NP], ACT.Tanh, 0.5).then_inc(s_ja, 1)
                    if b % 2:
                        hi(U_OF[("in", {"g1": 16, "g0": 12}[kind])] + b // 2 + 2)

            act.wait_ge(s_at, len(ITEMS))
            split_hi(lambda c: Z[:, c, :])
            u = U_OF[("fnet", 0)]
            act.wait_ge(s_job, J_OF[("fnet", 3)] + 1)
            hi(u + 2)
            act.wait_ge(s_job, J_OF[("fnet", 7)] + 1)
            hi(u + 3)
            gates("g1", "fnet", range(DC))
            for c in range(CB):
                act.copy(bh[:, c, 0:NP], Q[:, c, 0:NP])
                act.copy(bh[:, c, NP:T].rearrange("p (r n i) -> p r n i", r=ROWS, n=4), by_block(Q[:, c, NP:T])).then_inc(s_bh, 1)
            u = U_OF[("na", 0)]
            act.wait_ge(s_job, J_OF[("na", 3)] + 1)
            hi(u + 2)
            act.wait_ge(s_job, J_OF[("na", 7)] + 1)
            hi(u + 3)
            gates("g0", "na", range(0, 2))
            for c in range(CB):
                act.wait_ge(s_lnc, c + 1)
                act.activation(Yq[:, c, :], Yc[:, c, :], ACT.Square).then_inc(s_ysq, 1)
            gates("g0", "na", range(2, 6))
            for c in range(CB):
                act.wait_ge(s_yr, c + 1)
                act.activation(Yq[:, c, :], Yc[:, c, :], ACT.Tanh, bias=hlnb[:, 4 + c:5 + c], scale=hlnb[:, c:c + 1])
                act.activation(Yc[:, c, :], Yc[:, c, :], ACT.Identity, bias=colsT[:, 16 + c:17 + c],
                               scale=colsT[:, 12 + c:13 + c]).then_inc(s_yt, 1)
            gates("g0", "na", range(6, 8))
            for c in range(CB):
                act.wait_ge(s_yz, c + 1)
                act.copy(bh[:, c, :], Yc[:, c, :]).then_inc(s_bh, 1)
            u = U_OF[("conv", 0)]
            act.wait_ge(s_job, J_OF[("conv", 3)] + 1)
            hi(u + 2)
            act.wait_ge(s_bl, 3 * CB)
            for g in range(2):
                act.dma_start(g1bc[:, g, :], mods_d[g:g + 1, 0:D].to_broadcast([P, D])).then_inc(s_bc, 16)
                act.dma_start(sh2bc[:, g, :], mods_d[g:g + 1, D:2 * D].to_broadcast([P, D])).then_inc(s_bc, 16)
                act.dma_start(A2bc[:, g, :], mods_d[g:g + 1, 2 * D:3 * D].to_broadcast([P, D])).then_inc(s_bc, 16)
            act.dma_start(n2bc, a["norm2_g"].to_broadcast([P, D])).then_inc(s_bc, 16)
            act.dma_start(wr, a["w_router"][0].rearrange("(c p) e -> p c e", p=P)).then_inc(s_bc, 16)
            act.dma_start(br, a["b_router"]).then_inc(s_bc, 16)
            act.wait_ge(s_job, J_OF[("conv", 7)] + 1)
            hi(u + 3)
            act.wait_ge(s_gm, 2 * DC)
            act.dma_start(X[:, 0, :], a["x_prompt"][0]).then_inc(s_xr, 16)
            for t in range(4):
                act.dma_start(X[:, 1 + t, :], a["x_sample"][0, t * P:(t + 1) * P, :]).then_inc(s_xr, 16)
            for b in range(DC):
                act.copy(hTh[:, b, :], M[:, b, :]).then_inc(s_hh, 1)
            for i in range(2):
                act.wait_ge(s_job, J_OF[("out", i, 0)] + 1)
                hi(u + 4 + i)
            for i, t in enumerate(TILE_ORDER):
                act.wait_ge(s_x2, i + 1)
                act.activation(junk, X[:, t, :], ACT.Square, accum_out=stat[:, t:t + 1]).then_inc(s_q2, 1)
                act.wait_ge(s_q2, i + 1)

            def softmax_exp(i):
                act.wait_ge(s_mx2, i + 1)
                act.activation(aff[:, TILE_ORDER[i], :], lgs[:, i, :], ACT.Exp, bias=stat[:, 36 + i:37 + i],
                               accum_out=stat[:, 41 + i:42 + i]).then_inc(s_ex2, 1)

            def turned(i):
                for hf in range(2):
                    act.wait_ge(s_t2, 2 * i + hf + 1)
                    if i >= 2:
                        act.wait_ge(s_lg, i - 1)
                    act.copy(h2T[:, i % 2, 4 * hf:4 * hf + 4, :],
                             bank[4 + hf][:, :].rearrange("p (c t) -> p c t", c=4)).then_inc(s_t2e, 1)

            for i, t in enumerate(TILE_ORDER):
                act.wait_ge(s_h2, i + 1)
                act.dma_start(h2_d[t * P:(t + 1) * P, :], h2t[:, i % 2, :]).then_inc(s_hst[i % 2], 16)
                act.dma_start(acc_d[t * P:(t + 1) * P, :], X[:, t, :]).then_inc(s_xst, 16)
                turned(i)
                if i >= 1:
                    softmax_exp(i - 1)
            softmax_exp(TT - 1)
            act.wait_ge(s_route, 2)
            act.wait_ge(s_hst[0], 48)
            act.wait_ge(s_hst[1], 32)
            act.dma_start(g2r[0:CAP_S, :], mods_d[1:2, 3 * D:4 * D].to_broadcast([CAP_S, D])).then_inc(s_g2, 16)
            act.dma_start(g2r[CAP_S:M_E, :], mods_d[0:1, 3 * D:4 * D].to_broadcast([CAP_P, D])).then_inc(s_g2, 16)

            def e_hi_unit(e, k):
                act.wait_ge(e_w[k % 6], 32 * e + 16 * (k // 6) + 16)
                if not (isinstance(e, int) and e == 0 and k < 3):
                    act.wait_ge(e_unit, 12 * e + (k - 2))
                act.copy(h2r[:, k % 3, :], w2[:, k % 6, :]).then_inc(e_hi, 1)

            def x_hi(n):
                for hf in range(2):
                    act.wait_ge(e_xt, 2 * n + (hf + 1))
                    act.copy(xTh[:, 4 * hf:4 * hf + 4, :],
                             bank[6 + hf][:, 0:4 * M_E].rearrange("p (c t) -> p c t", c=4)).then_inc(e_xh, 1)

            def expert(e, last):
                for k in range(0, 6):
                    e_hi_unit(e, k)
                act.wait_ge(e_unit, 12 * e + 4)
                for hf in range(2):
                    act.activation(sg[:, 512 * hf:512 * hf + 512], bank[hf][0:M_E, :], ACT.Silu).then_inc(e_sg, 1)
                for k in range(6, 11):
                    e_hi_unit(e, k)
                if not last:
                    x_hi(e + 1)
                for hf in range(2):
                    act.wait_ge(e_ht, 2 * e + (hf + 1))
                    act.copy(hTh2[:, 4 * hf:4 * hf + 4, :],
                             bank[hf][:, 0:4 * M_E].rearrange("p (c t) -> p c t", c=4)).then_inc(e_hh, 1)
                e_hi_unit(e, 11)

            x_hi(0)
            expert(0, False)
            with act.Fori(1, E_N - 1) as e:
                expert(e, False)
            expert(E_N - 1, True)

            act.wait_ge(e_add, 16 * E_N)
            act.dma_start(fgbc, a["final_norm_g"].rearrange("(o d) -> o d", o=1).to_broadcast([P, D])).then_inc(s_fin, 16)
            for t in range(TT):
                act.dma_start(fin[:, t, :], acc_d[t * P:(t + 1) * P, :]).then_inc(s_fin, 16)
            act.wait_ge(s_fin, 16 * 6)
            for t in range(TT):
                act.activation(junk, fin[:, t, :], ACT.Square, accum_out=stat[:, t:t + 1]).then_inc(s_fq, 1)
                act.wait_ge(s_fq, t + 1)
            for t in range(TT):
                act.wait_ge(s_fy, t + 1)
                dst = y_prompt[0] if t == 0 else y_sample[0, (t - 1) * P:t * P, :]
                act.dma_start(dst, fin[:, t, :]).then_inc(s_out, 16)
            act.wait_ge(s_out, 16 * 7)

        @block.vector
        def _(dve):
            n_va = [0]

            def link(ins):
                n_va[0] += 1
                ins.then_inc(s_va, 1)
                dve.wait_ge(s_va, n_va[0])

            def lo(u):
                dve.wait_ge(s_hi, u + 1)
                dve.tensor_tensor(lring[:, u % 2, :], wring[:, u % 2, :], hring[:, u % 2, :].bitcast(F32),
                                  ALU.subtract).then_inc(s_lov, 1)

            taps = [(k, c) for k in range(CW) for c in range(CB)]
            tap = [0]

            def conv(n):
                for _ in range(n):
                    if tap[0] == len(taps):
                        return
                    k, c = taps[tap[0]]
                    if k == 0:
                        ins = dve.tensor_scalar(Y[:, c, :], U[:, c, 0:Y_N], cwT[:, c, 0:1], None, ALU.mult)
                    else:
                        dve.wait_ge(s_cv, tap[0] - CB + 1)
                        ins = dve.scalar_tensor_tensor(Y[:, c, :], U[:, c, k:k + Y_N], cwT[:, c, k:k + 1], Y[:, c, :],
                                                       ALU.mult, ALU.add)
                    ins.then_inc(s_cv, 1)
                    tap[0] += 1

            def ada_rows(i):
                dve.wait_ge(s_ada, i + 1)
                dve.tensor_copy(rows4[:, i % 2, :], bank[4 + i % 2][0:4, 0:256]).then_inc(s_rows4, 1)

            def ada_mod(i):
                dve.wait_ge(s_mrow, i + 1)
                dst = modrow[:, i % 2, :] if i < 8 else modall[:, (i - 8) * 256:(i - 7) * 256]
                dve.tensor_copy(dst, bank[7][0:2, 256:512]).then_inc(s_modrow, 1)

            def ada_col(i):
                dve.wait_ge(s_mcol, i + 1)
                dve.tensor_copy(modcol[:, 2 * i:2 * i + 2, :],
                                bank[6][:, 0:4].rearrange("p (c g) -> p c g", c=2)).then_inc(s_modcol, 1)

            dve.memset(c4[:, :, :].bitcast(F32), 0.0).then_inc(s_va, 1)
            n_va[0] += 1
            dve.memset(U, 0.0).then_inc(s_u0, 1)
            dve.wait_ge(s_turn, 1)
            dve.tensor_copy(colsT[:, :], bank[7][:, 16:36])
            dve.tensor_copy(cwT[:, :, :], bank[7][:, 64:64 + CB * CW].rearrange("p (c k) -> p c k", c=CB))
            dve.tensor_copy(kcT, bank[6][:, :].rearrange("p (c t) -> p c t", c=CB))
            dve.tensor_copy(cs, bank[7][:, 0:16]).then_inc(s_turned, 1)
            dve.wait_ge(s_turned, 1)
            dve.wait_ge(s_aa, 1)
            link(dve.scalar_tensor_tensor(cs3, cs2, 1.0, cs, ALU.add, ALU.mult))
            dve.tensor_scalar(cs3, cs3, 0.5, None, ALU.mult).then_inc(s_cast, 1)
            dve.wait_ge(s_c4, 1)
            dve.wait_ge(s_cast, 1)
            dve.tensor_tensor(c4[:, :, 2:4], cs3.rearrange("p (c g) -> p c g", g=2), c4[:, :, 0:2].bitcast(F32),
                              ALU.subtract).then_inc(s_cast, 1)
            lo(0); lo(1)
            dve.wait_ge(s_c4, 2)
            dve.tensor_tensor(gtab_l[:, :], graw, gtab_h[:, :].bitcast(F32), ALU.subtract).then_inc(s_cast, 1)
            dve.tensor_scalar(hlnb[:, 0:8], colsT[:, 12:20], 0.5, None, ALU.mult).then_inc(s_cast, 1)
            dve.wait_ge(s_rstd, 1)
            for t in range(TT):
                dve.tensor_scalar(X[:, t, :], X[:, t, :], stat[:, 10 + t:11 + t], None, ALU.mult).then_inc(s_xhat, 1)
            for i in range(8):
                ada_rows(i)
                if i + 2 < 8:
                    lo(i + 2)
                if i >= 1:
                    ada_mod(i - 1)
                if i >= 2:
                    ada_col(i - 2)
            ada_mod(7)
            ada_col(6)
            ada_col(7)
            dve.wait_ge(s_modcol, 8)
            dve.scalar_tensor_tensor(A1[:, :, :], modcol[:, DC:2 * DC, :], 1.0,
                                     colsT[:, 0:DC].unsqueeze(2).to_broadcast([P, DC, 2]), ALU.add, ALU.mult).then_inc(s_a1, 1)
            for dc in range(DC):
                dve.wait_ge(s_hh, dc + 1)
                dve.tensor_tensor(hTl[:, dc, :], tmp5[:, dc % 4, :], hTh[:, dc, :].bitcast(F32), ALU.subtract).then_inc(s_h, 1)
            for i in range(4):
                first = U_OF[("in", i)]
                base = 8 + 4 * i
                for j in range(4):
                    lo(first + 1 + j)
                    if j == 0 and i >= 2:
                        for b in (2 * i - 4, 2 * i - 3):
                            dve.wait_ge(s_ja, freed(J_OF[("u2", b + 4)])[1])
                            for lo_, n_, x0 in ((U_P, NP, 0), (U_S, NS, NP)):
                                ins = dve.scalar_tensor_tensor(U[:, b, lo_:lo_ + n_], tmp5[:, b % 2, x0:x0 + n_], 1.0,
                                                               U[:, b, lo_:lo_ + n_], ALU.add, ALU.mult)
                            ins.then_inc(s_u, 1)
                    if j >= 1:
                        ada_rows(base + j - 1)
                    if j >= 2:
                        ada_mod(base + j - 2)
                ada_rows(base + 3)
                ada_mod(base + 2)
                ada_mod(base + 3)
            dve.wait_ge(s_u, 4)
            for i in range(4):
                conv(6)
                n = J_OF[("f", i)]
                dve.wait_ge(s_fh, i + 1)
                bs, bp = job_bank(n)
                dve.tensor_tensor(bl[:, i, NP:T], bs, bh[:, i, NP:T].bitcast(F32), ALU.subtract)
                dve.tensor_tensor(bl[:, i, 0:NP], bp, bh[:, i, 0:NP].bitcast(F32), ALU.subtract).then_inc(s_jd, 1)

            def uv_lo(g):
                for t in range(TT):
                    n = J_OF[("uv", g, t)]
                    dve.wait_ge(s_uvh, TT * g + t + 1)
                    dve.tensor_tensor(uvl[:, g % 2, t, :], bank[n % 2][:, 0:256], uvh[:, g % 2, t, :].bitcast(F32),
                                      ALU.subtract).then_inc(s_jd, 1)

            uv_lo(0)
            for g in range(1, 4):
                uv_lo(g)
                conv(4)
            conv(50)
            dve.wait_ge(s_out, 32)
            for it in range(len(ITEMS) + 2):
                if it < len(ITEMS):
                    blk, h = ITEMS[it]
                    w = it % 2
                    kn = NP if blk < 0 else 384
                    dve.wait_ge(s_sc, it + 1)
                    if it >= 2:
                        dve.wait_ge(s_pt, it - 1)
                    sc = bank[4 + w]
                    if blk < 0:
                        dve.tensor_scalar(sp[:, w, 0:kn], sc[:, 0:kn], SCALE, None, ALU.mult).then_inc(s_ev, 1)
                    else:
                        dve.wait_ge(s_bm, it - 8 + 1)
                        dve.scalar_tensor_tensor(sp[:, w, 0:256], sc[:, 0:256], SCALE,
                                                 bm[:, w].rearrange("p r j -> p (r j)"), ALU.mult, ALU.add)
                        dve.tensor_scalar(sp[:, w, 256:384], sc[:, 256:384], SCALE, None, ALU.mult).then_inc(s_ev, 1)
                    dve.wait_ge(s_ev, it + 1)
                    dve.tensor_reduce(stat[:, 30 + w:31 + w], sp[:, w, 0:kn], AX, ALU.max, negate=True).then_inc(s_mx, 1)
                conv(2)
                if it < len(ITEMS):
                    dve.wait_ge(s_ex, it + 1)
                    link(dve.reciprocal(stat[:, 34 + w:35 + w], stat[:, 32 + w:33 + w]))
                    dve.tensor_scalar(sp[:, w, 0:kn], sp[:, w, 0:kn], stat[:, 34 + w:35 + w], None, ALU.mult).then_inc(s_pn, 1)
                if it >= 2:
                    j = it - 2
                    blk, h = ITEMS[j]
                    r0 = DH * (h % 2)
                    dve.wait_ge(s_pv, j + 1)
                    if blk < 0:
                        dve.tensor_copy(Q[r0:r0 + DH, h // 2, 0:NP], bank[7][r0:r0 + DH, 0:P]).then_inc(s_at, 1)
                    else:
                        dst = Q[r0:r0 + DH, h // 2, NP + P * blk:NP + P * (blk + 1)]
                        dve.tensor_copy(dst, bank[7][r0:r0 + DH, 0:P]).then_inc(s_at, 1)
            conv(len(taps))

            def split_lo(src, n0):
                for c in range(CB):
                    dve.wait_ge(s_bh, n0 + c + 1)
                    dve.tensor_tensor(bl[:, c, :], src(c), bh[:, c, :].bitcast(F32), ALU.subtract).then_inc(s_bl, 1)

            def product(kind, b):
                n = J_OF[(kind, b)]
                dve.wait_ge(s_job, n + 1)
                if b == 0:
                    dve.wait_ge(s_ja, freed(J_OF[({"fnet": "g2", "na": "g1", "conv": "g0"}[kind], 7)])[1])
                bs, bp = job_bank(n)
                dst = M if kind == "fnet" else G
                dve.scalar_tensor_tensor(dst[:, b, NP:T], G[:, b, NP:T], 1.0, bs, ALU.add, ALU.mult)
                dve.scalar_tensor_tensor(dst[:, b, 0:NP], G[:, b, 0:NP], 1.0, bp, ALU.add, ALU.mult).then_inc(s_jd, 1)

            split_lo(lambda c: Z[:, c, :], 0)
            for b in range(DC):
                product("fnet", b)
            for c in range(CB):
                dve.wait_ge(s_bh, CB + c + 1)
                dve.tensor_tensor(bl[:, c, 0:NP], Q[:, c, 0:NP], bh[:, c, 0:NP].bitcast(F32), ALU.subtract)
                tok = "p (r n i) -> p r n i"
                dve.tensor_tensor(bl[:, c, NP:T].rearrange(tok, r=ROWS, n=4), by_block(Q[:, c, NP:T]),
                                  bh[:, c, NP:T].rearrange(tok, r=ROWS, n=4).bitcast(F32), ALU.subtract).then_inc(s_bl, 1)
            dve.wait_ge(s_cv, len(taps))
            for c in range(CB):
                dve.tensor_scalar(Yc[:, c, 0:NP], Y[:, c, 0:NP], 0.5, colsT[:, 8 + c:9 + c], ALU.mult, ALU.add)
                dve.tensor_scalar(Yc[:, c, NP:T], Y[:, c, Y_S:Y_S + NS], 0.5, colsT[:, 8 + c:9 + c], ALU.mult,
                                  ALU.add).then_inc(s_yc, 1)
            n0 = freed(J_OF[("fnet", 7)])[1]
            for b in range(DC):
                product("na", b)
                dve.wait_ge(s_jd, n0 + b + 1)
                dve.tensor_tensor(M[:, b, :], M[:, b, :], G[:, b, :], ALU.add).then_inc(s_gm, 1)
            dve.wait_ge(s_ln, 1)
            link(dve.tensor_scalar(stat[:, 15:20], bank[7][:, 100:105], -1.0 / 512, None, ALU.mult))
            for t in range(TT):
                ins = dve.tensor_scalar(diag[:, t * P:(t + 1) * P], ident[:, :], stat[:, 15 + t:16 + t], None, ALU.mult)
            ins.then_inc(s_lnd, 1)
            dve.wait_ge(s_ln, 2)
            for c in range(CB):
                dve.tensor_tensor(Yc[:, c, NP:T], Yc[:, c, NP:T], bank[4][:, :], ALU.add)
                dve.tensor_tensor(Yc[:, c, 0:NP], Yc[:, c, 0:NP], bank[5][:, 0:P], ALU.add).then_inc(s_lnc, 1)
            dve.wait_ge(s_ln, 3)
            dve.tensor_scalar(stat[:, 20:25], bank[7][:, 110:115], 1.0 / 512, EPS, ALU.mult, ALU.add).then_inc(s_lns, 1)
            dve.wait_ge(s_lnr, 1)
            for t in range(TT):
                ins = dve.tensor_scalar(diag[:, t * P:(t + 1) * P], ident[:, :], stat[:, 25 + t:26 + t], None, ALU.mult)
            ins.then_inc(s_lnd, 1)
            dve.wait_ge(s_ln, 4)
            for c in range(CB):
                dve.tensor_tensor(Yc[:, c, NP:T], Yc[:, c, NP:T], bank[4][:, :], ALU.mult)
                dve.tensor_tensor(Yc[:, c, 0:NP], Yc[:, c, 0:NP], bank[5][:, 0:P], ALU.mult).then_inc(s_yr, 1)
            for c in range(CB):
                dve.wait_ge(s_yt, c + 1)
                dve.scalar_tensor_tensor(Yc[:, c, :], Yq[:, c, :], 1.0, Yc[:, c, :], ALU.add, ALU.mult).then_inc(s_yz, 1)
            dve.wait_ge(s_yz, CB)
            split_lo(lambda c: Yc[:, c, :], 2 * CB)
            n0 = freed(J_OF[("na", 7)])[1]
            for b in range(DC):
                product("conv", b)
                dve.wait_ge(s_jd, n0 + b + 1)
                dve.scalar_tensor_tensor(M[:, b, :], G[:, b, :], 0.5, M[:, b, :], ALU.mult, ALU.add).then_inc(s_gm, 1)
            for b in range(DC):
                dve.wait_ge(s_hh, DC + b + 1)
                dve.tensor_tensor(hTl[:, b, :], M[:, b, :], hTh[:, b, :].bitcast(F32), ALU.subtract).then_inc(s_h, 1)
            dve.wait_ge(s_bc, 16 * 9)
            for g in range(2):
                dve.scalar_tensor_tensor(A2bc[:, g, :], A2bc[:, g, :], 1.0, n2bc, ALU.add, ALU.mult).then_inc(s_a2, 1)
            dve.wait_ge(s_xr, 16 * 5)
            for i in range(4):
                for m, t in enumerate(TILE_ORDER):
                    n = J_OF[("out", i, t)]
                    g = 0 if t == 0 else 1
                    cols = slice(256 * i, 256 * i + 256)
                    dve.wait_ge(s_job, n + 1)
                    dve.scalar_tensor_tensor(otmp[:, n % 2, :], bank[n % 2][:, 0:256], 0.5, g1bc[:, g, cols], ALU.mult,
                                             ALU.mult).then_inc(s_jd, 1)
                    dve.wait_ge(s_jd, freed(n)[1])
                    ins = dve.tensor_tensor(X[:, t, cols], X[:, t, cols], otmp[:, n % 2, :], ALU.add)
                    ins.then_inc(s_x2 if i == 3 else s_xp, 1)
            dve.wait_ge(s_x2, TT)
            dve.wait_ge(s_a2, 2)

            def softmax(i):
                t = TILE_ORDER[i]
                dve.wait_ge(s_lg, i + 1)
                dve.tensor_copy(lgs[:, i, :], bank[7][:, 0:E_N]).then_inc(s_lgc, 1)
                dve.wait_ge(s_lgc, i + 1)
                dve.tensor_reduce(stat[:, 36 + i:37 + i], lgs[:, i, :], AX, ALU.max,
                                  negate=True).then_inc(s_mx2, 1)
                dve.wait_ge(s_ex2, i + 1)
                link(dve.reciprocal(stat[:, 46 + i:47 + i], stat[:, 41 + i:42 + i]))
                dve.tensor_scalar(aff[:, t, :], aff[:, t, :], stat[:, 46 + i:47 + i], None, ALU.mult).then_inc(s_aff, 1)

            for i, t in enumerate(TILE_ORDER):
                g = 0 if t == 0 else 1
                dve.wait_ge(s_r2, i + 1)
                if i >= 2:
                    dve.wait_ge(s_hst[i % 2], 16 * (i // 2))
                    dve.wait_ge(s_t2, 2 * i - 2)
                link(dve.scalar_tensor_tensor(h2t[:, i % 2, :], X[:, t, :], stat[:, 10 + t:11 + t], A2bc[:, g, :],
                                              ALU.mult, ALU.mult))
                dve.tensor_tensor(h2t[:, i % 2, :], h2t[:, i % 2, :], sh2bc[:, g, :], ALU.add).then_inc(s_h2, 1)
                if i >= 2:
                    softmax(i - 2)
            softmax(TT - 2)
            softmax(TT - 1)
            dve.wait_ge(s_affp, TT)
            dve.tensor_copy(affT[:, NP:T], bank[6][0:E_N, :])
            link(dve.tensor_copy(affT[:, 0:NP], bank[3][0:E_N, 0:P]))
            for x0, x1, v0, cap in ((NP, T, 0, CAP_S), (0, NP, CAP_S, CAP_P)):
                for r in range(cap // 8):
                    v = slice(v0 + 8 * r, v0 + 8 * r + 8)
                    link(dve.max(vals[:, v], affT[:, x0:x1]))
                    link(dve.max_index(idxu[:, v], vals[:, v], affT[:, x0:x1]))
                    link(dve.match_replace(affT[:, x0:x1], vals[:, v], affT[:, x0:x1], -1.0))
            dve.tensor_scalar(idxf[:, 0:CAP_S], idxu[:, 0:CAP_S], float(NP), None, ALU.add)
            dve.tensor_copy(idxf[:, CAP_S:M_E], idxu[:, CAP_S:M_E]).then_inc(s_idx, 1)
            dve.wait_ge(s_idxp, 1)
            dve.tensor_copy(idxT[:, :], bank[4][0:M_E, 0:E_N]).then_inc(s_route, 1)
            dve.tensor_copy(gateT[:, :], bank[4][0:M_E, E_N:2 * E_N]).then_inc(s_route, 1)
            dve.wait_ge(s_route, 2)
            dve.wait_ge(s_g2, 32)

            def e_lo_unit(e, k):
                dve.wait_ge(e_hi, 12 * e + (k + 1))
                dve.tensor_tensor(l2r[:, k % 3, :], w2[:, k % 6, :], h2r[:, k % 3, :].bitcast(F32),
                                  ALU.subtract).then_inc(e_lo, 1)

            def x_lo(e):
                for hf in range(2):
                    dve.wait_ge(e_xh, 2 * e + (hf + 1))
                    dve.tensor_tensor(xTl[:, 4 * hf:4 * hf + 4, :], bank[6 + hf][:, 0:4 * M_E].rearrange("p (c t) -> p c t", c=4),
                                      xTh[:, 4 * hf:4 * hf + 4, :].bitcast(F32), ALU.subtract).then_inc(e_xl, 1)

            def expert(e, last):
                first = isinstance(e, int) and e == 0
                for k in range(3, 10):
                    e_lo_unit(e, k)
                dve.wait_ge(e_unit, 12 * e + 8)
                for hf in range(2):
                    dve.wait_ge(e_sg, 2 * e + (hf + 1))
                    x = sg[:, 512 * hf:512 * hf + 512]
                    dve.tensor_tensor(x, x, bank[2 + hf][0:M_E, :], ALU.mult).then_inc(e_h, 1)
                e_lo_unit(e, 10)
                if not last:
                    x_lo(e + 1)
                for hf in range(2):
                    dve.wait_ge(e_hh, 2 * e + (hf + 1))
                    dve.tensor_tensor(hTl2[:, 4 * hf:4 * hf + 4, :], bank[hf][:, 0:4 * M_E].rearrange("p (c t) -> p c t", c=4),
                                      hTh2[:, 4 * hf:4 * hf + 4, :].bitcast(F32), ALU.subtract).then_inc(e_hl, 1)
                e_lo_unit(e, 11)
                if not last:
                    e_lo_unit(e + 1, 0)
                    e_lo_unit(e + 1, 1)
                dve.wait_ge(e_unit, 12 * e + 12)
                if not first:
                    dve.wait_ge(e_add, 16 * e)
                for hf in range(2):
                    x = slice(512 * hf, 512 * hf + 512)
                    dve.scalar_tensor_tensor(ye[:, x], bank[4 + hf][0:M_E, :], gateT[:, at(e)], g2r[:, x], ALU.mult,
                                             ALU.mult).then_inc(e_y, 1)
                if not last:
                    e_lo_unit(e + 1, 2)

            x_lo(0)
            for k in range(3):
                e_lo_unit(0, k)
            expert(0, False)
            with dve.Fori(1, E_N - 1) as e:
                expert(e, False)
            expert(E_N - 1, True)
            for t in range(TT):
                dve.wait_ge(s_fr, t + 1)
                dve.scalar_tensor_tensor(fin[:, t, :], fin[:, t, :], stat[:, 10 + t:11 + t], fgbc, ALU.mult,
                                         ALU.mult).then_inc(s_fy, 1)

        @block.tensor
        def _(pe):
            def mm3(out, lh, ll, rh, rl, start, stop):
                pe.matmul(out, lh, rh, start=start, stop=False)
                pe.matmul(out, lh, rl, start=False, stop=False)
                return pe.matmul(out, ll, rh, start=False, stop=stop)

            def bank_free(n):
                if n >= 2:
                    dve, count = freed(n - 2)
                    pe.wait_ge(s_jd if dve else s_ja, count)

            def slot(u):
                return unit_view(hring[:, u % 2, :], u), unit_view(lring[:, u % 2, :], u)

            def block_steps(n, u, c0, xh, xl, nk):
                wh, wl = slot(u)
                bs, bp = job_bank(n)
                for c in range(nk):
                    if c == 0:
                        bank_free(n)
                    a_h, a_l = wh[:, c, c0:c0 + P], wl[:, c, c0:c0 + P]
                    st, en = c == 0, c == nk - 1
                    pe.matmul(bs, a_h, xh[:, c, NP:T], start=st, stop=False)
                    pe.matmul(bp, a_h, xh[:, c, 0:NP], start=st, stop=False)
                    pe.matmul(bs, a_h, xl[:, c, NP:T], start=False, stop=False)
                    pe.matmul(bp, a_h, xl[:, c, 0:NP], start=False, stop=False)
                    pe.matmul(bs, a_l, xh[:, c, NP:T], start=False, stop=en)
                    last = pe.matmul(bp, a_l, xh[:, c, 0:NP], start=False, stop=en)
                    if en:
                        last.then_inc(s_job, 1)
                    yield last

            def run(steps):
                for _ in steps:
                    pass

            def in_block(kind, b):
                u = U_OF[("in", {"u2": 0, "q": 4, "k": 6, "f": 10, "g0": 12, "g1": 16, "g2": 20}[kind] + b // 2)]
                return block_steps(J_OF[(kind, b)], u, P * (b % 2), hTh, hTl, DC), u

            pe.wait_ge(s_cst, 16 * N_CST)
            for dc in range(DC):
                pe.transpose(bank[7][:, 2 * dc:2 * dc + 2], c2[:, dc * P:(dc + 1) * P], ident[0:2, 0:2])
            pe.transpose(bank[7][:, 16:36], rows20, ident[0:20, 0:20])
            for c in range(CB):
                pe.transpose(bank[7][:, 64 + CW * c:64 + CW * (c + 1)], cwr[:, c * P:(c + 1) * P], ident[0:CW, 0:CW])
            for c in range(CB):
                last = pe.transpose(bank[6][:, c * P:(c + 1) * P], kraw[:, c * P:(c + 1) * P], ident[:, :])
            last.then_inc(s_turn, 1)

            def ada(i):
                u = U_OF[("ada", i)]
                lo_ready(pe, u)
                if i >= 2:
                    pe.wait_ge(s_rows4, i - 1)
                wh, wl = slot(u)
                for dc in range(DC):
                    pe.matmul(bank[4 + i % 2][:, 0:256], c4[:, dc, :], wh[:, dc, :], start=dc == 0, stop=False)
                    last = pe.matmul(bank[4 + i % 2][:, 0:256], c4[:, dc, :], wl[:, dc, :], start=False, stop=dc == DC - 1)
                last.then_inc(s_ada, 1)

            def ada_sum(i):
                pe.wait_ge(s_rows4, i + 1)
                if i >= 1:
                    pe.wait_ge(s_modrow, i)
                pe.matmul(bank[7][0:2, 256:512], sel4[:, :], rows4[:, i % 2, :], start=True, stop=False)
                pe.matmul(bank[7][0:2, 256:512], ones[0:1, 0:2], brow[:, i * 256:(i + 1) * 256], start=False,
                          stop=True).then_inc(s_mrow, 1)

            def ada_turn(i):
                pe.wait_ge(s_modrow, i + 1)
                if i >= 1:
                    pe.wait_ge(s_modcol, i)
                for j in range(2):
                    last = pe.transpose(bank[6][:, 2 * j:2 * j + 2], modrow[:, i % 2, j * P:(j + 1) * P], ident[0:2, 0:2])
                last.then_inc(s_mcol, 1)

            pe.wait_ge(s_cast, 2)
            pe.wait_ge(s_turned, 1)
            for i in range(8):
                ada(i)
                if i >= 1:
                    ada_sum(i - 1)
                if i >= 2:
                    ada_turn(i - 2)
            ada_sum(7)
            ada_turn(6)
            ada_turn(7)
            pe.wait_ge(s_xhat, TT)
            for dc in range(DC):
                n = J_OF[("xT", dc)]
                bank_free(n)
                bs, bp = job_bank(n)
                for t in range(4):
                    pe.transpose(bs[:, t * P:(t + 1) * P], X[:, 1 + t, dc * P:(dc + 1) * P], ident[:, :])
                pe.transpose(bp, X[:, 0, dc * P:(dc + 1) * P], ident[:, :]).then_inc(s_job, 1)
            pe.wait_ge(s_h, DC)
            pe.wait_ge(s_modcol, 8)
            for i in range(4):
                for b in (2 * i, 2 * i + 1):
                    steps, u = in_block("u2", b)
                    lo_ready(pe, u)
                    run(steps)
                base = 8 + 4 * i
                for j in range(4):
                    ada(base + j)
                    if j >= 1:
                        ada_sum(base + j - 1)
                ada_sum(base + 3)
            for b in range(4):
                steps, u = in_block("f", b)
                lo_ready(pe, u)
                run(steps)

            def uv(g):
                for t in range(TT):
                    n = J_OF[("uv", g, t)]
                    bank_free(n)
                    x = slice(t * P, (t + 1) * P)
                    mm3(bank[n % 2][:, 0:256], bh[:, g, x], bl[:, g, x], gtab_h[:, 0:256], gtab_l[:, 0:256], True,
                        True).then_inc(s_job, 1)

            pe.wait_ge(s_jd, freed(J_OF[("f", 3)])[1])
            pe.wait_ge(s_cast, 4)
            uv(0)
            u = U_OF[("dft", 0)]
            (ch, cl), (sh, sl) = slot(u), slot(u + 1)
            for g in range(4):
                if g < 3:
                    uv(g + 1)
                if g == 0:
                    lo_ready(pe, u + 1)
                n = J_OF[("z", g)]
                pe.wait_ge(s_jd, freed(J_OF[("uv", g, TT - 1)])[1])
                bank_free(n)
                bs, bp = job_bank(n)
                w = g % 2
                for c in range(4):
                    mm3(bs, uvh[:, w, c + 1, 0:P], uvl[:, w, c + 1, 0:P], ch[:, c, :], cl[:, c, :], c == 0, False)
                    mm3(bs, uvh[:, w, c + 1, P:2 * P], uvl[:, w, c + 1, P:2 * P], sh[:, c, :], sl[:, c, :], False, c == 3)
                mm3(bp, uvh[:, w, 0, 0:P], uvl[:, w, 0, 0:P], gtab_h[:, 0:P], gtab_l[:, 0:P], True, False)
                mm3(bp, uvh[:, w, 0, P:2 * P], uvl[:, w, 0, P:2 * P], gtab_h[:, 2 * P:3 * P], gtab_l[:, 2 * P:3 * P],
                    False, True).then_inc(s_job, 1)
            for kind in ("q", "k"):
                for b in range(4):
                    steps, u = in_block(kind, b)
                    lo_ready(pe, u)
                    run(steps)

            def token_major(kind, i, t, u):
                n = J_OF[(kind, i, t)]
                bank_free(n)
                wh, wl = slot(u)
                x = slice(t * P, (t + 1) * P)
                for dc in range(DC):
                    last = mm3(bank[n % 2][:, 0:256], hTh[:, dc, x], hTl[:, dc, x], wh[:, dc, :], wl[:, dc, :], dc == 0,
                               dc == DC - 1)
                last.then_inc(s_job, 1)

            for i in range(2):
                u = U_OF[("in", 8 + i)]
                lo_ready(pe, u)
                for t in range(TT):
                    token_major("v", i, t, u)
            pe.wait_ge(s_ja, freed(J_OF[("k", 3)])[1])
            for c in range(4):
                last = pe.transpose(bank[6][:, c * P:(c + 1) * P], K[:, c, 0:NP], ident[:, :])
            last.then_inc(s_kt, 1)

            pe.wait_ge(s_ja, freed(J_OF[("v", 1, 4)])[1])
            pe.wait_ge(s_x, 16 * 6)
            pe.wait_ge(s_ko, 1)
            gate_steps = []
            for b in range(DC):
                steps, u = in_block("g2", b)
                gate_steps.append((steps, u))

            for it in range(len(ITEMS) + 2):
                if it < len(ITEMS):
                    blk, h = ITEMS[it]
                    r = slice(DH * (h % 2), DH * (h % 2) + DH)
                    hc = h // 2
                    sc = bank[4 + it % 2]
                    if it >= 2:
                        pe.wait_ge(s_ev, it - 1)
                    if blk < 0:
                        pe.matmul(sc[:, 0:P], Q[r, hc, 0:NP], K[r, hc, 0:NP], start=True, stop=True).then_inc(s_sc, 1)
                    else:
                        q = Q[r, hc, NP + P * blk:NP + P * (blk + 1)]
                        k = K[r, hc, NP:T].rearrange("p (r c) -> p r c", c=GW)[:, :, KB[blk]:KB[blk] + 32]
                        pe.matmul(sc[:, 0:256], q, k, start=True, stop=True)
                        pe.matmul(sc[:, 256:384], q, kcT[r, hc, :], start=True, stop=True).then_inc(s_sc, 1)
                    b, part = it // 5, it % 5
                    if part == 0:
                        lo_ready(pe, gate_steps[b][1])
                    for _ in range((2, 2, 2, 1, 1)[part]):
                        next(gate_steps[b][0])
                if 1 <= it <= len(ITEMS):
                    j = it - 1
                    blk = ITEMS[j][0]
                    pe.wait_ge(s_pn, j + 1)
                    if j >= 1:
                        pe.wait_ge(s_pte, j)
                    for c in range(1 if blk < 0 else 3):
                        last = pe.transpose(bank[6][:, c * P:(c + 1) * P], sp[:, j % 2, c * P:(c + 1) * P], ident[:, :])
                    last.then_inc(s_pt, 1)
                if it >= 2:
                    j = it - 2
                    blk, h = ITEMS[j]
                    pe.wait_ge(s_pte, j + 1)
                    if j >= 1:
                        pe.wait_ge(s_at, j)
                    if blk >= 0 and h == 0:
                        pe.wait_ge(s_vw[blk % 2], 32 * (blk // 2 + 1))
                    out = bank[7][DH * (h % 2):DH * (h % 2) + DH, 0:P]
                    cols = slice(DH * h, DH * h + DH)
                    vals_ = [vp[:, cols]] if blk < 0 else [vw[:, blk % 2, 0, cols], vw[:, blk % 2, 1, cols], vc[:, cols]]
                    for c, v in enumerate(vals_):
                        last = pe.matmul(out, v, pT[:, j % 2, c * P:(c + 1) * P], start=c == 0, stop=c == len(vals_) - 1)
                    last.then_inc(s_pv, 1)

            def branch(kind, n_split):
                for b in range(DC):
                    u = U_OF[(kind, b // 4)]
                    if b % 4 == 0:
                        lo_ready(pe, u)
                    if b == 0:
                        pe.wait_ge(s_bl, n_split)
                    run(block_steps(J_OF[(kind, b)], u, P * (b % 4), bh, bl, CB))

            def gate(kind, b):
                steps, u = in_block(kind, b)
                lo_ready(pe, u)
                run(steps)

            def ln_sums(src, col):
                for t in range(TT):
                    for c in range(CB):
                        last = pe.matmul(bank[7][:, col + t:col + t + 1], src[:, c, t * P:(t + 1) * P], ones[:, 0:1],
                                         start=c == 0, stop=c == CB - 1)
                last.then_inc(s_ln, 1)

            def ln_spread(n):
                pe.wait_ge(s_lnd, n)
                pe.matmul(bank[4][:, :], ones[:, :], diag[:, NP:T], start=True, stop=True)
                pe.matmul(bank[5][:, 0:P], ones[:, :], diag[:, 0:NP], start=True, stop=True).then_inc(s_ln, 1)

            branch("fnet", CB)
            for b in range(DC):
                gate("g1", b)
            branch("na", 2 * CB)
            pe.wait_ge(s_yc, CB)
            ln_sums(Yc, 100)
            for b in range(DC):
                gate("g0", b)
                if b == 1:
                    ln_spread(1)
                if b == 3:
                    pe.wait_ge(s_ysq, CB)
                    ln_sums(Yq, 110)
                if b == 5:
                    ln_spread(2)
            branch("conv", 3 * CB)
            pe.wait_ge(s_h, 2 * DC)
            for i in range(4):
                u = U_OF[("out", i)]
                lo_ready(pe, u)
                for t in TILE_ORDER:
                    token_major("out", i, t, u)

            def turn2(i):
                pe.wait_ge(s_h2, i + 1)
                if i >= 1:
                    pe.wait_ge(s_t2e, 2 * i)
                for hf in range(2):
                    for c in range(4):
                        dc = 4 * hf + c
                        last = pe.transpose(bank[4 + hf][:, c * P:(c + 1) * P], h2t[:, i % 2, dc * P:(dc + 1) * P], ident[:, :])
                    last.then_inc(s_t2, 1)

            def route(i):
                pe.wait_ge(s_t2e, 2 * i + 2)
                pe.wait_ge(s_bc, 16 * 9)
                if i >= 1:
                    pe.wait_ge(s_lgc, i)
                out = bank[7][:, 0:E_N]
                for dc in range(DC):
                    pe.matmul(out, h2T[:, i % 2, dc, :], wr[:, dc, :], start=dc == 0, stop=False)
                pe.matmul(out, ones[0:1, :], br, start=False, stop=True).then_inc(s_lg, 1)

            def turn_aff(i):
                t = TILE_ORDER[i]
                pe.wait_ge(s_aff, i + 1)
                dst = bank[3][0:E_N, 0:P] if t == 0 else bank[6][0:E_N, (t - 1) * P:t * P]
                pe.transpose(dst, aff[:, t, :], ident[:, :]).then_inc(s_affp, 1)

            for i in range(TT):
                turn2(i)
                route(i)
                if i >= 2:
                    turn_aff(i - 2)
            turn_aff(TT - 2)
            turn_aff(TT - 1)
            pe.wait_ge(s_idx, 1)
            pe.transpose(bank[4][0:M_E, 0:E_N], idxf, ident[0:E_N, 0:E_N])
            pe.transpose(bank[4][0:M_E, E_N:2 * E_N], vals, ident[0:E_N, 0:E_N]).then_inc(s_idxp, 1)

            def turn_tokens(e):
                pe.wait_ge(e_x, 16 * e + 16)
                for hf in range(2):
                    for c in range(4):
                        dc = 4 * hf + c
                        last = pe.transpose(bank[6 + hf][:, c * M_E:(c + 1) * M_E], xe[:, dc * P:(dc + 1) * P],
                                            ident[0:M_E, 0:M_E])
                    last.then_inc(e_xt, 1)

            def e_unit_mm(e, k, b0, xh, xl):
                pe.wait_ge(e_lo, 12 * e + (k + 1))
                wh = h2r[:, k % 3, :].rearrange("p (c n) -> p c n", c=2)
                wl = l2r[:, k % 3, :].rearrange("p (c n) -> p c n", c=2)
                q = k % 4
                for c in range(2):
                    for hf in range(2):
                        n = slice(512 * hf, 512 * hf + 512)
                        last = mm3(bank[b0 + hf][0:M_E, :], xh[:, 2 * q + c, :], xl[:, 2 * q + c, :], wh[:, c, n], wl[:, c, n],
                                   q == 0 and c == 0, q == 3 and c == 1)
                last.then_inc(e_unit, 1)

            def expert(e, last):
                first = isinstance(e, int) and e == 0
                pe.wait_ge(e_xl, 2 * e + 2)
                for k in range(8):
                    e_unit_mm(e, k, 0 if k < 4 else 2, xTh, xTl)
                if not last:
                    turn_tokens(e + 1)
                for hf in range(2):
                    pe.wait_ge(e_h, 2 * e + (hf + 1))
                    for c in range(4):
                        fc = 4 * hf + c
                        ins = pe.transpose(bank[hf][:, c * M_E:(c + 1) * M_E], sg[:, fc * P:(fc + 1) * P], ident[0:M_E, 0:M_E])
                    ins.then_inc(e_ht, 1)
                if not first:
                    pe.wait_ge(e_y, 2 * e)
                for k in range(8, 12):
                    if k % 2 == 0:
                        pe.wait_ge(e_hl, 2 * e + (1 if k == 8 else 2))
                    e_unit_mm(e, k, 4, hTh2, hTl2)

            turn_tokens(0)
            expert(0, False)
            with pe.Fori(1, E_N - 1) as e:
                expert(e, False)
            expert(E_N - 1, True)


_INS = ["x_prompt", "x_sample", "cache_k", "cache_v", "c", "c_ctx", "w_ada", "b_ada", "norm1_g", "w_in", "conv_w", "conv_b",
        "conv_ln_g", "conv_ln_b", "w_conv_out", "rpb", "w_na_out", "w_fnet", "w_out", "norm2_g", "w_router", "b_router",
        "w_e_gate", "w_e_up", "w_e_down", "final_norm_g"]
_OUTS = [(1, NP, D), (1, NS, D), (1, 1, NP, H, DH), (1, 1, NP, H, DH)]
_SCRATCH = [("mods", (2, 4 * D)), ("rpbpad", (16, RPL)), ("vals", (NS, 512)), ("h2", (T, D)), ("acc", (T, D))]


def shape_constants():
    p = np.arange(P)
    ang = 2 * np.pi * np.outer(p, p) / P
    dft_g = np.concatenate([np.cos(ang), -np.sin(ang), np.sin(ang)], axis=1) / np.sqrt(P)
    ll, kk = np.arange(NS), np.arange(NS)
    ang = 2 * np.pi * (np.outer(ll, kk) % NS) / NS
    dft_l = np.stack([np.cos(ang), np.sin(ang)]) / np.sqrt(NS)
    dft_l = dft_l.reshape(2, 4, P, NS).transpose(0, 2, 1, 3)
    i, j = np.arange(16)[:, None], np.arange(32)[None, :]
    mask = []
    for blk in (0, 1, 3):
        col, key = 16 * blk + i, KB[blk] + j
        start = np.clip(col - 8, 0, GW - 16)
        mask.append(np.where((key >= start) & (key < start + 16), 0.0, -1e30))
    mask = np.tile(np.stack(mask, axis=1), (8, 1, 1))
    sel4 = np.array([[1, 0], [0, 1], [1, 0], [0, 1]])
    made = {"ident": np.eye(P), "ones": np.ones((P, P)), "dft_g": dft_g, "dft_l": dft_l, "mask": mask, "sel4": sel4}
    return {k: np.ascontiguousarray(v, dtype=np.float32) for k, v in made.items()}


def kernel(**inputs):
    import concourse.bacc as _bacc
    from concourse.bass_utils import run_bass_kernel_spmd as _run

    nc = _bacc.Bacc("TRN2", target_bir_lowering=False, num_devices=1)
    arrays, a = {}, {}
    for name in _INS:
        x = np.ascontiguousarray(inputs[name])
        arrays["in_" + name] = x
        a[name] = nc.dram_tensor("in_" + name, x.shape, F32, kind="ExternalInput").ap()
    consts = {}
    for name, x in shape_constants().items():
        arrays["const_" + name] = x
        consts[name] = nc.dram_tensor("const_" + name, x.shape, F32, kind="ExternalInput").ap()
    outs = [nc.dram_tensor(f"out_{i}", s, F32, kind="ExternalOutput").ap() for i, s in enumerate(_OUTS)]
    scratch = [nc.dram_tensor("scratch_" + n, s, F32, kind="Internal").ap() for n, s in _SCRATCH]
    trunk(nc, a, outs, consts, scratch)
    r = _run(nc, [arrays], core_ids=[0])
    return tuple(r.results[0][f"out_{i}"] for i in range(len(_OUTS)))
```

```python
from contextlib import ExitStack

import numpy as np
import concourse.bass as bass
from concourse import mybir

F32 = mybir.dt.float32
F32R = mybir.dt.float32r
U32 = mybir.dt.uint32
ALU = mybir.AluOpType
ACT = mybir.ActivationFunctionType
AX = mybir.AxisListType.X

P = 128
D = 1024
DC = D // P
NP, NS = 128, 512
T = NP + NS
TT = T // P
TH = T // 2
H, DH = 8, 64
GW = 64
ROWS = NS // GW
R0 = ((NP + NS) // 2 - NP) // GW
CW = 31
PADW = CW // 2
CB = 4
E_N = 16
FE = 1024
CAP_S, CAP_P = 2 * NS // E_N, 2 * NP // E_N
M_E = CAP_S + CAP_P
EPS = 1e-6
UN = 2048
SCALE = DH ** -0.5
BW = 48
RPL = 32 + 120 * BW
U_P, U_S = PADW, PADW + NP + PADW
U_N = U_S + NS + PADW
Y_S = U_S - PADW
Y_N = Y_S + NS

UNITS = [("ada", i) for i in range(8)]
for _i in range(4):
    UNITS += [("in", _i)] + [("ada", 8 + 4 * _i + _j) for _j in range(4)]
UNITS += [("in", 10), ("in", 11), ("dft", 0), ("dft", 1)]
UNITS += [("in", i) for i in range(4, 10)]
UNITS += [("in", i) for i in range(20, 24)] + [("fnet", 0), ("fnet", 1)]
UNITS += [("in", i) for i in range(16, 20)] + [("na", 0), ("na", 1)]
UNITS += [("in", i) for i in range(12, 16)] + [("conv", 0), ("conv", 1)]
UNITS += [("out", i) for i in range(4)]
U_OF = {u: n for n, u in enumerate(UNITS)}
N_U = len(UNITS)


def lo_count(engine, n):
    return sum((UNITS[i][0] == "ada") == (engine == "dve") for i in range(n))


JOBS = [("xT", i) for i in range(DC)]
JOBS += [("u2", i) for i in range(8)]
JOBS += [("f", i) for i in range(4)]
JOBS += [("uv", 0, t) for t in range(TT)]
for _g in range(4):
    if _g < 3:
        JOBS += [("uv", _g + 1, t) for t in range(TT)]
    JOBS += [("z", _g)]
JOBS += [("q", i) for i in range(4)] + [("k", i) for i in range(4)]
JOBS += [("v", u, t) for u in range(2) for t in range(TT)]
JOBS += [("g2", i) for i in range(DC)] + [("fnet", i) for i in range(DC)]
JOBS += [("g1", i) for i in range(DC)] + [("na", i) for i in range(DC)]
JOBS += [("g0", i) for i in range(DC)] + [("conv", i) for i in range(DC)]
TILE_ORDER = [1, 2, 3, 4, 0]
JOBS += [("out", u, t) for u in range(4) for t in TILE_ORDER]
IN_JOBS = [("u2", 0), ("q", 4), ("k", 6), ("v", 8), ("f", 10), ("g0", 12), ("g1", 16), ("g2", 20)]
J_OF = {j: n for n, j in enumerate(JOBS)}
BY_DVE = ("f", "uv", "fnet", "na", "conv", "out")


def freed(n):
    dve = JOBS[n][0] in BY_DVE
    return dve, sum((JOBS[i][0] in BY_DVE) == dve for i in range(n + 1))


EXPERT_UNITS = [("w_e_gate", 0, 0), ("w_e_gate", 0, 1), ("w_e_up", 0, 0), ("w_e_up", 0, 1),
                ("w_e_gate", 1, 0), ("w_e_gate", 1, 1), ("w_e_up", 1, 0), ("w_e_up", 1, 1)]
EXPERT_UNITS += [("w_e_down", None, q) for q in range(4)]


def expert_unit(k):
    name, ch, r = EXPERT_UNITS[k]
    if ch is None:
        return name, slice(256 * r, 256 * r + 256), slice(0, D)
    return name, slice(512 * r, 512 * r + 512), slice(512 * ch, 512 * ch + 512)


ITEMS = [(-1, h) for h in range(H)] + [(n, h) for n in range(4) for h in range(H)]


def gate_step(it):
    return DC * (DC - 1) * it // len(ITEMS)


KB = [0, 8, 24, 32]
VARIANT = [0, 1, 1, 2]
U_OFF = [16, 8, 8, 0]


def trunk(nc, a, outs, consts, scratch):
    y_prompt, y_sample, new_k, new_v = outs
    mods_d, rpb_d, v_d, h2_d, acc_d = scratch

    w_in = a["w_in"][0].rearrange("(c p) n -> p c n", p=P)
    w_ada = a["w_ada"][0].rearrange("(c p) n -> p c n", p=P)
    w_br = {"fnet": a["w_fnet"][0], "na": a["w_na_out"][0], "conv": a["w_conv_out"][0]}
    w_out = a["w_out"][0].rearrange("(c p) n -> p c n", p=P)

    def unit_src(u):
        kind, i = UNITS[u]
        if kind == "ada":
            return w_ada[:, :, i * 256:(i + 1) * 256]
        if kind == "in":
            return w_in[:, :, i * 256:(i + 1) * 256]
        if kind == "dft":
            return consts["dft_l"][i]
        if kind == "out":
            return w_out[:, :, i * 256:(i + 1) * 256]
        return w_br[kind].rearrange("(c p) n -> p c n", p=P)[:, :, i * 512:(i + 1) * 512]

    def unit_view(x, u):
        c = CB if UNITS[u][0] in ("fnet", "na", "conv", "dft") else DC
        return x.rearrange("p (c n) -> p c n", c=c)

    with ExitStack() as ctx:
        def sem(name):
            return ctx.enter_context(nc.semaphore(name))

        def place(stack, name, shape, dt=F32):
            return stack.enter_context(nc.sbuf_tensor(name, shape, dt))

        ident = place(ctx, "ident", [P, P])
        ones = place(ctx, "ones", [P, P])
        gtab_h = place(ctx, "gtab_h", [P, 384], F32R)
        gtab_l = place(ctx, "gtab_l", [P, 384], F32R)
        mask = place(ctx, "mask", [P, 3, 32])
        sel4 = place(ctx, "sel4", [4, 2])
        cwT = place(ctx, "cwT", [P, CB, CW])
        colsT = place(ctx, "colsT", [P, 20])
        modcol = place(ctx, "modcol", [P, 16, 2])
        A1 = place(ctx, "A1", [P, DC, 2])
        stat = place(ctx, "stat", [P, 52])
        half = place(ctx, "half", [P, 8])
        hlnb = place(ctx, "hlnb", [P, 8])
        idxT = place(ctx, "idxT", [M_E, E_N], U32)
        gateT = place(ctx, "gateT", [M_E, E_N])
        idx_g = place(ctx, "idx_g", [M_E, 1], U32)
        idx_s = place(ctx, "idx_s", [M_E, 1], U32)

        with ExitStack() as p1:
            wring = place(p1, "wring", [P, 2, UN])
            hring = place(p1, "hring", [P, 2, UN], F32R)
            lring = place(p1, "lring", [P, 2, UN], F32R)
            hTh = place(p1, "hTh", [P, DC, T], F32R)
            hTl = place(p1, "hTl", [P, DC, T], F32R)
            with ExitStack() as t0:
                tmp5 = place(t0, "tmp5", [P, 4, T])
                c4 = place(t0, "c4", [P, DC, P], F32R)
            with ExitStack() as t1:
                vw = place(t1, "vw", [P, 2, 2, 512])
                bm = place(t1, "bm", [P, 2, 8, 32])
                sp = place(t1, "sp", [P, 2, 384])
                pT = place(t1, "pT", [P, 2, 384])
            bh = place(p1, "bh", [P, CB, T], F32R)
            bl = place(p1, "bl", [P, CB, T], F32R)
            with ExitStack() as t2:
                uvh = place(t2, "uvh", [P, 2, TT, 256], F32R)
                uvl = place(t2, "uvl", [P, 2, TT, 256], F32R)
            xg_f = place(p1, "xg_f", [P, TT * D])
            with ExitStack() as t3:
                place(t3, "before", [P, 2560])
                h3 = place(t3, "h3", [P, UN], F32R)
                l3 = place(t3, "l3", [P, UN], F32R)
            fa = place(p1, "fa", [P, 17648])
        X = xg_f[:, :].rearrange("p (t d) -> p t d", t=TT)
        G = xg_f[:, :].rearrange("p (b t) -> p b t", b=DC)
        kst = xg_f[:, 2048:2560]
        Vs = xg_f[:, 0:2048].rearrange("p (t d) -> p t d", t=4)
        Z = fa[:, 0:2560].rearrange("p (c t) -> p c t", c=CB)
        Q = fa[:, 2560:5120].rearrange("p (c t) -> p c t", c=CB)
        K = fa[:, 5120:7680].rearrange("p (c t) -> p c t", c=CB)
        Bt = fa[:, 7680:10752].rearrange("p (h r u) -> p h r u", h=H, r=8)
        M = fa[:, 5120:10240].rearrange("p (b t) -> p b t", b=DC)
        U = fa[:, 10752:10752 + CB * U_N].rearrange("p (c t) -> p c t", c=CB)
        Y = fa[:, 13492:13492 + CB * Y_N].rearrange("p (c t) -> p c t", c=CB)
        SM = 16112
        kcT = fa[:, SM:SM + 512].rearrange("p (c t) -> p c t", c=CB)
        vc = fa[:, SM + 512:SM + 1024]
        vp = fa[:, SM + 1024:SM + 1536]
        rows4 = fa[0:4, 0:512].rearrange("p (b n) -> p b n", b=2)
        modrow = fa[0:2, 512:1024].rearrange("p (b n) -> p b n", b=2)
        modall = xg_f[0:2, 0:4 * D]
        bias24 = fa[0:24, 1600:1856]
        pick24 = fa[0:24, 1856:1904].rearrange("p (u g) -> p u g", g=2)
        c2 = fa[0:2, 13492:13492 + D]
        rows20 = fa[0:20, 14516:14516 + P]
        cwr = fa[0:CW, 14644:14644 + 512]
        kraw = fa[:, 15156:15156 + 512]
        graw = fa[:, 1024:1408]
        cs = fa[:, 1408:1424]
        cs2 = fa[:, 1424:1440]
        cs3 = fa[:, 1440:1456]
        rpad = fa[0:120, 1536:1536 + BW]
        Yc = fa[:, 10752:13312].rearrange("p (c t) -> p c t", c=CB)
        Yq = fa[:, 13492:16052].rearrange("p (c t) -> p c t", c=CB)
        diag = fa[:, 0:640]
        X2 = fa[:, 0:TT * D].rearrange("p (t d) -> p t d", t=TT)
        g1bc = fa[:, 10752:12800].rearrange("p (g d) -> p g d", g=2)
        A2bc = xg_f[:, 0:2048].rearrange("p (g d) -> p g d", g=2)
        sh2bc = fa[:, 12800:14848].rearrange("p (g d) -> p g d", g=2)
        n2bc = fa[:, 14848:15872]
        otmp = xg_f[:, 2048:2560].rearrange("p (b n) -> p b n", b=2)
        h2t = fa[:, 5120:7168].rearrange("p (b d) -> p b d", b=2)
        h2T = fa[:, 7168:9216].rearrange("p (b c t) -> p b c t", b=2, c=DC)
        junk = fa[:, 9216:10240]
        wr = fa[:, SM + 1040:SM + 1168].rearrange("p (c e) -> p c e", c=DC)
        br = fa[0:1, SM + 1168:SM + 1184]
        lgs = fa[:, SM + 960:SM + 1040].rearrange("p (t e) -> p t e", t=TT)
        aff = fa[:, SM + 880:SM + 960].rearrange("p (t e) -> p t e", t=TT)
        affT = fa[0:E_N, SM:SM + T]
        vals = fa[0:E_N, SM + 640:SM + 720]
        idxf = fa[0:E_N, SM + 720:SM + 800]
        idxu = fa[0:E_N, SM + 800:SM + 880].bitcast(U32)

        with ExitStack() as p2:
            w2 = place(p2, "w2", [P, 12, UN])
            h2r = place(p2, "h2r", [P, 3, UN], F32R)
            l2r = place(p2, "l2r", [P, 3, UN], F32R)
            xe = place(p2, "xe", [M_E, D])
            xTh = place(p2, "xTh", [P, DC, M_E], F32R)
            xTl = place(p2, "xTl", [P, DC, M_E], F32R)
            sg = place(p2, "sg", [M_E, D])
            hTh2 = place(p2, "hTh2", [P, DC, M_E], F32R)
            hTl2 = place(p2, "hTl2", [P, DC, M_E], F32R)
            ye = place(p2, "ye", [M_E, D])
            g2r = place(p2, "g2r", [M_E, D])
        fin = xg_f[:, :].rearrange("p (t d) -> p t d", t=TT)
        fgbc = fa[:, 10752:11776]

        bank = [ctx.enter_context(nc.psum_tensor(f"bank{i}", [P, 512], F32)) for i in range(8)]

        def job_bank(n):
            return bank[n % 2][:, :], bank[2 + n % 2][:, 0:P]

        def job_halves(n):
            return (slice(0, TH), bank[n % 2][:, 0:TH]), (slice(TH, T), bank[2 + n % 2][:, 0:TH])

        s_cst = sem("s_cst"); s_x = sem("s_x"); s_cast = sem("s_cast")
        s_rpad = sem("s_rpad"); s_rpb1 = sem("s_rpb1"); s_rpb2 = sem("s_rpb2"); s_bt = sem("s_bt")
        s_w = [sem(f"s_w{i}") for i in range(5)]
        s_hi = sem("s_hi"); s_lov = sem("s_lov"); s_lop = sem("s_lop")
        s_job = sem("s_job"); s_ja = sem("s_ja"); s_jd = sem("s_jd")
        s_turn = sem("s_turn"); s_turned = sem("s_turned"); s_c4 = sem("s_c4")
        s_ada = sem("s_ada"); s_rows4 = sem("s_rows4"); s_mrow = sem("s_mrow"); s_modrow = sem("s_modrow")
        s_mcol = sem("s_mcol"); s_modcol = sem("s_modcol"); s_modst = sem("s_modst")
        s_ssq = sem("s_ssq"); s_rstd = sem("s_rstd"); s_xhat = sem("s_xhat")
        s_a1 = sem("s_a1"); s_hh = sem("s_hh"); s_h = sem("s_h")
        s_tb = sem("s_tb"); s_u = sem("s_u"); s_fh = sem("s_fh"); s_uvh = sem("s_uvh")
        s_cv = sem("s_cv"); s_vst = sem("s_vst"); s_vw = [sem("s_vwa"), sem("s_vwb")]
        s_kt = sem("s_kt"); s_ko = sem("s_ko"); s_out = sem("s_out")
        s_sc = sem("s_sc"); s_bm = sem("s_bm"); s_ev = sem("s_ev"); s_mx = sem("s_mx"); s_ex = sem("s_ex")
        s_pn = sem("s_pn"); s_pt = sem("s_pt"); s_pte = sem("s_pte"); s_pv = sem("s_pv"); s_at = sem("s_at")
        s_bh = sem("s_bh"); s_bl = sem("s_bl")
        s_ln = sem("s_ln"); s_lnd = sem("s_lnd"); s_lnc = sem("s_lnc"); s_lns = sem("s_lns"); s_lnr = sem("s_lnr"); s_yc = sem("s_yc"); s_ysq = sem("s_ysq")
        s_yr = sem("s_yr"); s_yt = sem("s_yt"); s_yz = sem("s_yz")
        s_bc = sem("s_bc"); s_x2 = sem("s_x2"); s_xr = sem("s_xr")
        s_q2 = sem("s_q2"); s_r2 = sem("s_r2"); s_h2 = sem("s_h2"); s_hst = [sem("s_hsta"), sem("s_hstb")]; s_xst = sem("s_xst")
        s_t2 = sem("s_t2"); s_t2e = sem("s_t2e"); s_lg = sem("s_lg"); s_lgc = sem("s_lgc"); s_mx2 = sem("s_mx2"); s_ex2 = sem("s_ex2")
        s_aff = sem("s_aff"); s_affp = sem("s_affp"); s_idx = sem("s_idx"); s_idxp = sem("s_idxp")
        s_route = sem("s_route"); s_va = sem("s_va"); s_gm = sem("s_gm"); s_a2 = sem("s_a2"); s_xp = sem("s_xp"); s_u0 = sem("s_u0"); s_aa = sem("s_aa"); s_pa = sem("s_pa")
        e_w = [sem(f"e_w{i}") for i in range(12)]; s_bc2 = sem("s_bc2")
        e_hi = sem("e_hi"); e_lo = sem("e_lo"); e_unit = sem("e_unit")
        e_col = sem("e_col"); e_x = sem("e_x"); e_xt = sem("e_xt"); e_xh = sem("e_xh"); e_xl = sem("e_xl")
        e_sg = sem("e_sg"); e_h = sem("e_h"); e_ht = sem("e_ht"); e_hh = sem("e_hh"); e_hl = sem("e_hl")
        e_y = sem("e_y"); e_cs = sem("e_cs"); e_add = sem("e_add"); s_g2 = sem("s_g2")
        s_fin = [sem(f"s_fin{i}") for i in range(TT)]; s_fg = sem("s_fg"); s_fq = sem("s_fq"); s_fr = sem("s_fr"); s_fy = sem("s_fy")

        N_CST = 15

        def at(e):
            return slice(e, e + 1) if isinstance(e, int) else bass.ds(e, 1)

        block = ctx.enter_context(nc.Block())

        def by_block(x):
            return x.rearrange("p (n r i) -> p r n i", n=4, r=ROWS)

        EARLY = U_OF[("ada", 23)] + 1
        raw_slots = [wring[:, 0, :], wring[:, 1, :], fa[:, 8704:8704 + UN], fa[:, 6656:6656 + UN], fa[:, 13492:13492 + UN]]
        SLOT = [u % 5 if u < EARLY else u % 2 for u in range(N_U)]
        H_SLOT = [u % 3 if u < U_OF[("in", 4)] else u % 2 for u in range(N_U)]

        def split(u):
            k = H_SLOT[u]
            return (h3[:, :], l3[:, :]) if k == 2 else (hring[:, k, :], lring[:, k, :])

        def raw(u):
            return raw_slots[SLOT[u]]

        def fills(u):
            return SLOT[:u + 1].count(SLOT[u])

        def unit_used(eng, u):
            kind, i = UNITS[u]
            if kind == "ada":
                eng.wait_ge(s_ada, i + 1)
                return
            last = {"in": ("in", i), "dft": ("z", 3), "out": ("out", i, 0)}.get(kind, (kind, 4 * i + 3))
            if kind == "in":
                name, first = [(n, f) for n, f in IN_JOBS if f <= i][-1]
                last = (name, i - first, TT - 1) if name == "v" else (name, 2 * (i - first) + 1)
            eng.wait_ge(s_job, J_OF[last] + 1)

        def lo_ready(eng, u):
            if UNITS[u][0] == "ada":
                eng.wait_ge(s_lov, lo_count("dve", u + 1))
            else:
                eng.wait_ge(s_lop, lo_count("pool", u + 1))

        @block.sync
        def _(sp):
            def unit(u):
                earlier = [v for v in range(u) if SLOT[v] == SLOT[u]]
                if earlier:
                    lo_ready(sp, earlier[-1])
                elif SLOT[u] == 4:
                    sp.wait_ge(s_turn, 1)
                sp.dma_start(unit_view(raw(u), u), unit_src(u)).then_inc(s_w[SLOT[u]], 16)

            unit(0)
            for dst, src in ((ident[:, :], consts["ident"]), (c2[0:1, :], a["c_ctx"].rearrange("(o d) -> o d", o=1)),
                             (c2[1:2, :], a["c"]), (cwr, a["conv_w"][0]),
                             (kraw, a["cache_k"][0, 0].rearrange("l h d -> l (h d)"))):
                sp.dma_start(dst, src).then_inc(s_cst, 16)
            for r0, src in ((0, a["norm1_g"][0]), (8, a["conv_b"][0]), (12, a["conv_ln_g"][0]), (16, a["conv_ln_b"][0])):
                n = src.shape[0] // P
                sp.dma_start(rows20[r0:r0 + n, :], src.rearrange("(c p) -> c p", p=P)).then_inc(s_cst, 16)
            for dst, src in ((ones[:, :], consts["ones"]), (sel4[:, :], consts["sel4"]), (bias24, a["b_ada"].rearrange("o (u n) -> (o u) n", n=256)),
                             (pick24, consts["pick"]),
                             (graw, consts["dft_g"]), (mask[:, :, :], consts["mask"])):
                sp.dma_start(dst, src).then_inc(s_cst, 16)
            for u in range(1, 5):
                unit(u)
            sp.dma_start(X[:, 0, :], a["x_prompt"][0]).then_inc(s_x, 16)
            for t in range(4):
                sp.dma_start(X[:, 1 + t, :], a["x_sample"][0, t * P:(t + 1) * P, :]).then_inc(s_x, 16)
            sp.dma_start(vc, a["cache_v"][0, 0].rearrange("l h d -> l (h d)")).then_inc(s_x, 16)
            for u in range(5, N_U):
                unit(u)
            unit_used(sp, N_U - 1)

            def expert(e):
                for k in range(12):
                    name, rows, cols = expert_unit(k)
                    src = a[name][0, at(e), rows, cols].rearrange("o (c p) n -> p (o c) n", p=P)
                    if not (isinstance(e, int) and e == 0):
                        sp.wait_ge(e_lo, 12 * e + (k - 11))
                    sp.dma_start(w2[:, k, :].rearrange("p (c n) -> p c n", n=src.shape[2]), src).then_inc(e_w[k], 16)

            expert(0)
            with sp.Fori(1, E_N) as e:
                expert(e)

        @block.gpsimd
        def _(gp):
            gp.memset(rpad, 0.0).then_inc(s_rpad, 1)
            gp.memset(half[:, :], -0.5).then_inc(s_pa, 1)
            gp.wait_ge(s_rpad, 1)
            gp.dma_start(rpb_d[:, 0:32], rpad[0:16, 0:32]).then_inc(s_rpb1, 16)
            gp.wait_ge(s_rpb1, 16)
            gp.dma_start(rpad[:, 0:31], a["rpb"][0].rearrange("h a b -> (h a) b")).then_inc(s_rpb1, 16)
            gp.wait_ge(s_rpb1, 32)
            gp.dma_start(bass.AP(rpb_d.tensor, 16, [[BW, 120], [RPL + 1, 16], [1, BW]]),
                         rpad.unsqueeze(1).to_broadcast([120, 16, BW])).then_inc(s_rpb2, 16)
            gp.wait_ge(s_ssq, TT)
            gp.tensor_scalar(stat[:, 5:10], stat[:, 0:5], 1.0 / D, EPS, ALU.mult, ALU.add).then_inc(s_pa, 1)
            gp.wait_ge(s_pa, 2)
            gp.tensor_tensor(stat[:, 10:15], stat[:, 5:10], half[:, 0:5], ALU.pow).then_inc(s_rstd, 1)

            def lo(u):
                gp.wait_ge(s_hi, u + 1)
                gp.tensor_tensor(split(u)[1], raw(u), split(u)[0].bitcast(F32),
                                 ALU.subtract).then_inc(s_lop, 1)

            todo = [u for u in range(N_U) if UNITS[u][0] != "ada"]
            at_attention = todo.index(U_OF[("in", 20)])
            for u in todo[:6]:
                lo(u)
            gp.wait_ge(s_rpb2, 16)
            gp.wait_ge(s_modst, 16)
            for r in range(8):
                src = bass.AP(rpb_d.tensor, 16 + (7 - r) * BW - 1, [[RPL, 16], [15 * BW, H], [1, 8 * BW]])
                gp.dma_start(Bt[16 * r:16 * r + 16].rearrange("p h r u -> p h (r u)"), src).then_inc(s_bt, 16)
            for u in todo[6:at_attention]:
                lo(u)
            rest = todo[at_attention:]
            gp.wait_ge(s_bt, 16 * 8)
            n = 0
            for it, (blk, h) in enumerate(ITEMS):
                if it % 8 == 0 and n < 4:
                    lo(rest[n])
                    n += 1
                if blk < 0:
                    continue
                w = it - 8
                if w >= 2:
                    gp.wait_ge(s_ev, it - 1)
                o = U_OFF[blk]
                gp.tensor_tensor(bm[:, w % 2], Bt[:, h, :, o:o + 32],
                                 mask[:, VARIANT[blk], :].unsqueeze(1).to_broadcast([P, 8, 32]), ALU.add).then_inc(s_bm, 1)
            ln = U_OF[("in", 16)] - U_OF[("in", 20)] + 3
            for u in rest[n:ln]:
                lo(u)
            gp.wait_ge(s_lns, 1)
            gp.tensor_tensor(stat[:, 25:30], stat[:, 20:25], half[:, 0:5], ALU.pow).then_inc(s_lnr, 1)
            for u in rest[ln:]:
                lo(u)
            for i, t in enumerate(TILE_ORDER):
                gp.wait_ge(s_q2, i + 1)
                gp.tensor_scalar(stat[:, 5 + t:6 + t], stat[:, t:t + 1], 1.0 / D, EPS, ALU.mult, ALU.add).then_inc(s_pa, 1)
                gp.wait_ge(s_pa, 3 + i)
                gp.tensor_tensor(stat[:, 10 + t:11 + t], stat[:, 5 + t:6 + t], half[:, 0:1], ALU.pow).then_inc(s_r2, 1)
            for k in range(3):
                gp.wait_ge(e_hi, k + 1)
                gp.tensor_tensor(l2r[:, k, :], w2[:, k, :], h2r[:, k, :].bitcast(F32), ALU.subtract).then_inc(e_lo, 1)
            gp.wait_ge(s_route, 2)
            for st in (s_hst[0], s_hst[1], s_xst):
                gp.wait_ge(st, 16 * {id(s_hst[0]): 3, id(s_hst[1]): 2}.get(id(st), 5))

            def step():
                gp.tensor_tensor(half[0:1, 7:8], half[0:1, 5:6], half[0:1, 6:7], ALU.add)

            def gather(e):
                gp.tensor_copy(idx_g[:, :], idxT[:, at(e)]).then_inc(e_col, 1)
                gp.wait_ge(e_col, e + 1)
                step()
                gp.indirect_dma_start(xe[:, :], None, h2_d, bass.IndirectOffsetOnAxis(idx_g[:, 0:1], 0)).then_inc(e_x, 16)

            gather(0)

            def expert(e, last):
                if not last:
                    gp.wait_ge(e_xt, 2 * e + 2)
                    gather(e + 1)
                if not (isinstance(e, int) and e == 0):
                    gp.wait_ge(e_add, 16 * e)
                gp.tensor_copy(idx_s[:, :], idxT[:, at(e)]).then_inc(e_cs, 1)
                gp.wait_ge(e_cs, e + 1)
                gp.wait_ge(e_y, 2 * e + 2)
                step()
                gp.indirect_dma_start(acc_d, bass.IndirectOffsetOnAxis(idx_s[:, 0:1], 0), ye[:, :], None,
                                      compute_op=ALU.add).then_inc(e_add, 16)

            expert(0, False)
            with gp.Fori(1, E_N - 1) as e:
                expert(e, False)
            expert(E_N - 1, True)
            for t in range(TT):
                gp.wait_ge(s_fq, t + 1)
                gp.tensor_scalar(stat[:, 5 + t:6 + t], stat[:, t:t + 1], 1.0 / D, EPS, ALU.mult, ALU.add).then_inc(s_pa, 1)
                gp.wait_ge(s_pa, 8 + t)
                gp.tensor_tensor(stat[:, 10 + t:11 + t], stat[:, 5 + t:6 + t], half[:, 0:1], ALU.pow).then_inc(s_fr, 1)

        @block.scalar
        def _(act):
            def hi(u):
                act.wait_ge(s_w[SLOT[u]], 16 * fills(u))
                earlier = [v for v in range(u) if H_SLOT[v] == H_SLOT[u]]
                if earlier:
                    unit_used(act, earlier[-1])
                act.copy(split(u)[0], raw(u)).then_inc(s_hi, 1)

            def take(n, out, func=ACT.Copy, scale=1.0):
                act.wait_ge(s_job, n + 1)
                for t, b in job_halves(n):
                    ins = act.activation(out[:, t], b, func, scale=scale)
                return ins

            hi(0)
            act.wait_ge(s_turned, 1)
            act.activation(cs2, cs, ACT.Tanh, scale=0.5).then_inc(s_aa, 1)
            act.wait_ge(s_cast, 1)
            act.copy(c4[:, :, 0:2], cs3.rearrange("p (c g) -> p c g", g=2)).then_inc(s_c4, 1)
            act.copy(gtab_h[:, :], graw).then_inc(s_c4, 1)
            for u in range(1, 6):
                hi(u)
            act.wait_ge(s_x, 16 * 6)
            for t in range(TT):
                act.activation(tmp5[:, 0:2, :].rearrange("p a b -> p (a b)")[:, 0:D], X[:, t, :], ACT.Square,
                               accum_out=stat[:, t:t + 1]).then_inc(s_ssq, 1)
                act.wait_ge(s_ssq, t + 1)
            for u in range(6, 11):
                hi(u)
            act.wait_ge(s_a1, 1)
            for dc in range(DC):
                n = J_OF[("xT", dc)]
                act.wait_ge(s_job, n + 1)
                if dc >= 4:
                    act.wait_ge(s_h, dc - 3)
                bs, bp = job_bank(n)
                o = tmp5[:, dc % 4, :]
                act.activation(o[:, NP:T], bs, ACT.Identity, bias=modcol[:, dc, 1:2], scale=A1[:, dc, 1:2])
                act.activation(o[:, 0:NP], bp, ACT.Identity, bias=modcol[:, dc, 0:1], scale=A1[:, dc, 0:1]).then_inc(s_ja, 1)
                act.wait_ge(s_ja, dc + 1)
                act.copy(hTh[:, dc, :], o).then_inc(s_hh, 1)
            act.wait_ge(s_u0, 1)
            for i in range(4):
                first = U_OF[("in", i)]
                for b in (2 * i, 2 * i + 1):
                    n = J_OF[("u2", b)]
                    if b < 4:
                        act.wait_ge(s_job, n + 1)
                        (_, b0), (_, b1) = job_halves(n)
                        act.copy(U[:, b, U_P:U_P + NP], b0[:, 0:NP])
                        act.copy(U[:, b, U_S:U_S + TH - NP], b0[:, NP:TH])
                        act.copy(U[:, b, U_S + TH - NP:U_S + NS], b1).then_inc(s_ja, 1)
                    else:
                        if b >= 6:
                            act.wait_ge(s_u, b - 5)
                        o = tmp5[:, b % 2, :]
                        take(n, o, ACT.Tanh, 0.5).then_inc(s_ja, 1)
                for u in range(first + 3, first + 8):
                    hi(u)
            act.wait_ge(s_modrow, 24)
            act.dma_start(mods_d, modall).then_inc(s_modst, 16)
            act.wait_ge(s_u, 4)
            for i in range(4):
                if i == 2:
                    hi(U_OF[("dft", 1)])
                n = J_OF[("f", i)]
                act.wait_ge(s_job, n + 1)
                for t, b in job_halves(n):
                    ins = act.copy(bh[:, i, t], b)
                ins.then_inc(s_fh, 1)

            def uv_hi(g):
                for t in range(TT):
                    n = J_OF[("uv", g, t)]
                    act.wait_ge(s_job, n + 1)
                    act.copy(uvh[:, g % 2, t, :], bank[n % 2][:, 0:256]).then_inc(s_uvh, 1)

            act.wait_ge(s_modst, 16)
            uv_hi(0)
            for g in range(4):
                if g < 3:
                    uv_hi(g + 1)
                n = J_OF[("z", g)]
                act.wait_ge(s_job, n + 1)
                bs, bp = job_bank(n)
                act.copy(Z[:, g, NP:T], bs)
                act.copy(Z[:, g, 0:NP], bp).then_inc(s_ja, 1)
            u = U_OF[("in", 4)]
            hi(u); hi(u + 1)
            for kind, dst, base in (("q", Q, u), ("k", K, u + 2)):
                for b in range(4):
                    n = J_OF[(kind, b)]
                    if kind == "q":
                        act.wait_ge(s_job, n + 1)
                        (_, b0), (_, b1) = job_halves(n)
                        tok = "p (r n i) -> p r n i"
                        act.copy(Q[:, b, 0:NP], b0[:, 0:NP])
                        act.copy(by_block(Q[:, b, NP:T])[:, 0:R0], b0[:, NP:TH].rearrange(tok, r=R0, n=4))
                        act.copy(by_block(Q[:, b, NP:T])[:, R0:ROWS], b1.rearrange(tok, r=ROWS - R0, n=4)).then_inc(s_ja, 1)
                    else:
                        take(n, dst[:, b, :]).then_inc(s_ja, 1)
                    if b % 2:
                        hi(base + 2 + b // 2)
            for i in range(2):
                for t in range(TT):
                    n = J_OF[("v", i, t)]
                    act.wait_ge(s_job, n + 1)
                    dst = vp[:, i * 256:(i + 1) * 256] if t == 0 else Vs[:, t - 1, i * 256:(i + 1) * 256]
                    act.copy(dst, bank[n % 2][:, 0:256]).then_inc(s_ja, 1)
                hi(u + 6 + i)
            act.wait_ge(s_kt, 1)
            act.copy(kst, bank[6][:, :]).then_inc(s_ko, 1)
            act.wait_ge(s_ko, 1)
            act.dma_start(new_k.rearrange("b l s h d -> (b l s) (h d)"), kst).then_inc(s_out, 16)
            act.dma_start(new_v.rearrange("b l s h d -> (b l s) (h d)"), vp).then_inc(s_out, 16)
            act.dma_start(v_d.rearrange("(t p) d -> p t d", p=P), Vs).then_inc(s_vst, 16)

            def window_values(blk):
                for c in range(2):
                    src = bass.AP(v_d.tensor, (4 * c * GW + KB[blk]) * 512, [[GW * 512, 4], [512, 32], [1, 512]])
                    act.dma_start(vw[:, blk % 2, c, :], src).then_inc(s_vw[blk % 2], 16)

            hi_next = U_OF[("in", 22)]
            for it in range(len(ITEMS) + 2):
                if it < len(ITEMS):
                    blk, h = ITEMS[it]
                    w = it % 2
                    kn = NP if blk < 0 else 384
                    act.wait_ge(s_mx, it + 1)
                    act.activation(sp[:, w, 0:kn], sp[:, w, 0:kn], ACT.Exp, bias=stat[:, 30 + w:31 + w],
                                   accum_out=stat[:, 32 + w:33 + w]).then_inc(s_ex, 1)
                if 1 <= it <= len(ITEMS):
                    j = it - 1
                    blk, h = ITEMS[j]
                    kn = NP if blk < 0 else 384
                    act.wait_ge(s_pt, j + 1)
                    if j >= 2:
                        act.wait_ge(s_pv, j - 1)
                    act.copy(pT[:, j % 2, 0:kn], bank[6][:, 0:kn]).then_inc(s_pte, 1)
                if it == 3:
                    act.wait_ge(s_vst, 16)
                    act.wait_ge(s_out, 32)
                    window_values(0); window_values(1)
                if it >= 2 and ITEMS[it - 2] in ((0, 7), (1, 7)):
                    act.wait_ge(s_pv, it - 1)
                    window_values(ITEMS[it - 2][0] + 2)
                b = gate_step(it + 1) // DC - 1
                if it < len(ITEMS) and b >= 0 and gate_step(it) < DC * (b + 1):
                    n = J_OF[("g2", b)]
                    take(n, G[:, b, :], ACT.Tanh, 0.5).then_inc(s_ja, 1)
                    if b % 2:
                        hi(hi_next); hi_next += 1

            def split_hi(src):
                for c in range(CB):
                    act.copy(bh[:, c, :], src(c)).then_inc(s_bh, 1)

            def gates(kind, first, blocks):
                for b in blocks:
                    n = J_OF[(kind, b)]
                    if first == "fnet":
                        act.wait_ge(s_jd, freed(J_OF[(first, b)])[1])
                    else:
                        act.wait_ge(s_gm, b + 1)
                    take(n, G[:, b, :], ACT.Tanh, 0.5).then_inc(s_ja, 1)
                    if b % 2:
                        hi(U_OF[("in", {"g1": 16, "g0": 12}[kind])] + b // 2 + 2)

            act.wait_ge(s_at, len(ITEMS))
            split_hi(lambda c: Z[:, c, :])
            take(J_OF[("g2", DC - 1)], G[:, DC - 1, :], ACT.Tanh, 0.5).then_inc(s_ja, 1)
            hi(U_OF[("fnet", 1)])
            u = U_OF[("fnet", 0)]
            act.wait_ge(s_job, J_OF[("fnet", 3)] + 1)
            hi(u + 2)
            act.wait_ge(s_job, J_OF[("fnet", 7)] + 1)
            hi(u + 3)
            gates("g1", "fnet", range(0, 2))
            for c in range(CB):
                act.wait_ge(s_lnc, c + 1)
                act.activation(Yq[:, c, :], Yc[:, c, :], ACT.Square).then_inc(s_ysq, 1)
            gates("g1", "fnet", range(2, 6))
            for c in range(CB):
                act.copy(bh[:, c, 0:NP], Q[:, c, 0:NP])
                act.copy(bh[:, c, NP:T].rearrange("p (r n i) -> p r n i", r=ROWS, n=4), by_block(Q[:, c, NP:T])).then_inc(s_bh, 1)
            for c in range(CB):
                act.wait_ge(s_yr, c + 1)
                act.activation(Yq[:, c, :], Yc[:, c, :], ACT.Tanh, bias=hlnb[:, 4 + c:5 + c], scale=hlnb[:, c:c + 1])
                act.activation(Yc[:, c, :], Yc[:, c, :], ACT.Identity, bias=colsT[:, 16 + c:17 + c],
                               scale=colsT[:, 12 + c:13 + c]).then_inc(s_yt, 1)
            gates("g1", "fnet", range(6, 8))
            u = U_OF[("na", 0)]
            act.wait_ge(s_job, J_OF[("na", 3)] + 1)
            hi(u + 2)
            act.wait_ge(s_job, J_OF[("na", 7)] + 1)
            hi(u + 3)
            gates("g0", "na", range(0, 4))
            for c in range(CB):
                act.wait_ge(s_yz, c + 1)
                act.copy(bh[:, c, :], Yc[:, c, :]).then_inc(s_bh, 1)
            act.dma_start(X2[:, 0, :], a["x_prompt"][0]).then_inc(s_xr, 16)
            for t in range(4):
                act.dma_start(X2[:, 1 + t, :], a["x_sample"][0, t * P:(t + 1) * P, :]).then_inc(s_xr, 16)
            gates("g0", "na", range(4, 8))
            act.wait_ge(s_bl, 3 * CB)
            for g in range(2):
                act.dma_start(g1bc[:, g, :], mods_d[g:g + 1, 0:D].to_broadcast([P, D])).then_inc(s_bc, 16)
                act.dma_start(sh2bc[:, g, :], mods_d[g:g + 1, D:2 * D].to_broadcast([P, D])).then_inc(s_bc, 16)
            act.dma_start(n2bc, a["norm2_g"].to_broadcast([P, D])).then_inc(s_bc, 16)
            u = U_OF[("conv", 0)]
            act.wait_ge(s_job, J_OF[("conv", 3)] + 1)
            hi(u + 2)
            for b in range(DC - 1):
                act.wait_ge(s_gm, DC + b + 1)
                act.copy(hTh[:, b, :], M[:, b, :]).then_inc(s_hh, 1)
            act.wait_ge(s_job, J_OF[("conv", 7)] + 1)
            act.wait_ge(s_gm, 2 * DC)
            act.copy(hTh[:, DC - 1, :], M[:, DC - 1, :]).then_inc(s_hh, 1)
            hi(u + 3)
            for g in range(2):
                act.dma_start(A2bc[:, g, :], mods_d[g:g + 1, 2 * D:3 * D].to_broadcast([P, D])).then_inc(s_bc2, 16)
            act.dma_start(wr, a["w_router"][0].rearrange("(c p) e -> p c e", p=P)).then_inc(s_bc2, 16)
            act.dma_start(br, a["b_router"]).then_inc(s_bc2, 16)
            for i in range(2):
                act.wait_ge(s_job, J_OF[("out", i, 0)] + 1)
                hi(u + 4 + i)

            def softmax_exp(i):
                act.wait_ge(s_mx2, i + 1)
                act.activation(aff[:, TILE_ORDER[i], :], lgs[:, i, :], ACT.Exp, bias=stat[:, 36 + i:37 + i],
                               accum_out=stat[:, 41 + i:42 + i]).then_inc(s_ex2, 1)

            def turned(i):
                for hf in range(2):
                    act.wait_ge(s_t2, 2 * i + hf + 1)
                    if i >= 2:
                        act.wait_ge(s_lg, i - 1)
                    act.copy(h2T[:, i % 2, 4 * hf:4 * hf + 4, :],
                             bank[4 + hf][:, :].rearrange("p (c t) -> p c t", c=4)).then_inc(s_t2e, 1)

            for i in range(TT + 1):
                if i < TT:
                    act.wait_ge(s_x2, i + 1)
                    act.activation(junk, X2[:, TILE_ORDER[i], :], ACT.Square,
                                   accum_out=stat[:, TILE_ORDER[i]:TILE_ORDER[i] + 1]).then_inc(s_q2, 1)
                    act.wait_ge(s_q2, i + 1)
                if i >= 1:
                    t = TILE_ORDER[i - 1]
                    act.wait_ge(s_h2, i)
                    act.dma_start(h2_d[t * P:(t + 1) * P, :], h2t[:, (i - 1) % 2, :]).then_inc(s_hst[(i - 1) % 2], 16)
                    act.dma_start(acc_d[t * P:(t + 1) * P, :], X2[:, t, :]).then_inc(s_xst, 16)
                    turned(i - 1)
                if i >= 2:
                    softmax_exp(i - 2)
            act.wait_ge(s_hst[0], 48)
            act.wait_ge(s_hst[1], 32)
            act.wait_ge(s_xst, 16 * TT)
            act.dma_start(fgbc, a["final_norm_g"].rearrange("(o d) -> o d", o=1).to_broadcast([P, D])).then_inc(s_fg, 16)
            act.dma_start(g2r[0:CAP_S, :], mods_d[1:2, 3 * D:4 * D].to_broadcast([CAP_S, D])).then_inc(s_g2, 16)
            act.dma_start(g2r[CAP_S:M_E, :], mods_d[0:1, 3 * D:4 * D].to_broadcast([CAP_P, D])).then_inc(s_g2, 16)

            def e_hi_unit(e, k):
                act.wait_ge(e_w[k], 16 * e + 16)
                if not (isinstance(e, int) and e == 0 and k < 3):
                    act.wait_ge(e_unit, 12 * e + (k - 2))
                act.copy(h2r[:, k % 3, :], w2[:, k, :]).then_inc(e_hi, 1)

            def x_hi(n):
                for hf in range(2):
                    act.wait_ge(e_xt, 2 * n + (hf + 1))
                    act.copy(xTh[:, 4 * hf:4 * hf + 4, :],
                             bank[6 + hf][:, 0:4 * M_E].rearrange("p (c t) -> p c t", c=4)).then_inc(e_xh, 1)

            def silu(e, hf):
                act.wait_ge(e_unit, 12 * e + (4 * hf + 2))
                if not (isinstance(e, int) and e == 0) and hf == 0:
                    act.wait_ge(e_ht, 2 * e)
                act.activation(sg[:, 512 * hf:512 * hf + 512], bank[hf][0:M_E, :], ACT.Silu).then_inc(e_sg, 1)

            def h_hi(e, hf):
                act.wait_ge(e_ht, 2 * e + (hf + 1))
                act.copy(hTh2[:, 4 * hf:4 * hf + 4, :],
                         bank[hf][:, 0:4 * M_E].rearrange("p (c t) -> p c t", c=4)).then_inc(e_hh, 1)

            def expert(e, last):
                e_hi_unit(e, 4)
                silu(e, 0)
                for k in (5, 6, 7):
                    e_hi_unit(e, k)
                h_hi(e, 0)
                e_hi_unit(e, 8)
                silu(e, 1)
                e_hi_unit(e, 9)
                e_hi_unit(e, 10)
                h_hi(e, 1)
                e_hi_unit(e, 11)
                if not last:
                    e_hi_unit(e + 1, 0)
                    x_hi(e + 1)
                    for k in (1, 2, 3):
                        e_hi_unit(e + 1, k)

            for k in range(3):
                e_hi_unit(0, k)
            softmax_exp(TT - 1)
            x_hi(0)
            e_hi_unit(0, 3)
            expert(0, False)
            with act.Fori(1, E_N - 1) as e:
                expert(e, False)
            expert(E_N - 1, True)

            act.wait_ge(e_add, 16 * E_N)
            for t in range(TT):
                act.dma_start(fin[:, t, :], acc_d[t * P:(t + 1) * P, :]).then_inc(s_fin[t], 16)
            for t in range(TT):
                act.wait_ge(s_fin[t], 16)
                act.activation(junk, fin[:, t, :], ACT.Square, accum_out=stat[:, t:t + 1]).then_inc(s_fq, 1)
                act.wait_ge(s_fq, t + 1)
            for t in range(TT):
                act.wait_ge(s_fy, t + 1)
                dst = y_prompt[0] if t == 0 else y_sample[0, (t - 1) * P:t * P, :]
                act.dma_start(dst, fin[:, t, :]).then_inc(s_out, 16)
            act.wait_ge(s_out, 16 * 7)

        @block.vector
        def _(dve):
            n_va = [0]

            def link(ins):
                n_va[0] += 1
                ins.then_inc(s_va, 1)
                dve.wait_ge(s_va, n_va[0])

            def lo(u):
                dve.wait_ge(s_hi, u + 1)
                dve.tensor_tensor(split(u)[1], raw(u), split(u)[0].bitcast(F32),
                                  ALU.subtract).then_inc(s_lov, 1)

            taps = [(k, c) for k in range(CW) for c in range(CB)]
            tap = [0]

            def conv(n):
                for _ in range(n):
                    if tap[0] == len(taps):
                        return
                    k, c = taps[tap[0]]
                    if k == 0:
                        ins = dve.tensor_scalar(Y[:, c, :], U[:, c, 0:Y_N], cwT[:, c, 0:1], None, ALU.mult)
                    else:
                        dve.wait_ge(s_cv, tap[0] - CB + 1)
                        ins = dve.scalar_tensor_tensor(Y[:, c, :], U[:, c, k:k + Y_N], cwT[:, c, k:k + 1], Y[:, c, :],
                                                       ALU.mult, ALU.add)
                    ins.then_inc(s_cv, 1)
                    tap[0] += 1

            def ada_rows(i):
                dve.wait_ge(s_ada, i + 1)
                dve.tensor_copy(rows4[:, i % 2, :], bank[4 + i % 2][0:4, 0:256]).then_inc(s_rows4, 1)

            def ada_mod(i):
                dve.wait_ge(s_mrow, i + 1)
                dst = modrow[:, i % 2, :] if i < 8 else modall[:, (i - 8) * 256:(i - 7) * 256]
                dve.tensor_copy(dst, bank[7][0:2, 256:512]).then_inc(s_modrow, 1)

            def ada_col(i):
                dve.wait_ge(s_mcol, i + 1)
                dve.tensor_copy(modcol[:, 2 * i:2 * i + 2, :],
                                bank[6][:, 0:4].rearrange("p (c g) -> p c g", c=2)).then_inc(s_modcol, 1)

            dve.memset(c4[:, :, :].bitcast(F32), 0.0).then_inc(s_va, 1)
            n_va[0] += 1
            dve.memset(U, 0.0).then_inc(s_u0, 1)
            dve.wait_ge(s_turn, 1)
            dve.tensor_copy(colsT[:, :], bank[7][:, 16:36])
            dve.tensor_copy(cwT[:, :, :], bank[7][:, 64:64 + CB * CW].rearrange("p (c k) -> p c k", c=CB))
            dve.tensor_copy(kcT, bank[6][:, :].rearrange("p (c t) -> p c t", c=CB))
            dve.tensor_copy(cs, bank[7][:, 0:16]).then_inc(s_turned, 1)
            dve.wait_ge(s_turned, 1)
            dve.wait_ge(s_aa, 1)
            link(dve.scalar_tensor_tensor(cs3, cs2, 1.0, cs, ALU.add, ALU.mult))
            dve.tensor_scalar(cs3, cs3, 0.5, None, ALU.mult).then_inc(s_cast, 1)
            dve.wait_ge(s_c4, 1)
            dve.wait_ge(s_cast, 1)
            dve.tensor_tensor(c4[:, :, 2:4], cs3.rearrange("p (c g) -> p c g", g=2), c4[:, :, 0:2].bitcast(F32),
                              ALU.subtract).then_inc(s_cast, 1)
            lo(0); lo(1)
            dve.wait_ge(s_c4, 2)
            dve.tensor_tensor(gtab_l[:, :], graw, gtab_h[:, :].bitcast(F32), ALU.subtract).then_inc(s_cast, 1)
            dve.tensor_scalar(hlnb[:, 0:8], colsT[:, 12:20], 0.5, None, ALU.mult).then_inc(s_cast, 1)
            for i in range(8):
                ada_rows(i)
                if i == 6:
                    dve.wait_ge(s_rstd, 1)
                    for t in range(TT):
                        dve.tensor_scalar(X[:, t, :], X[:, t, :], stat[:, 10 + t:11 + t], None, ALU.mult).then_inc(s_xhat, 1)
                if i + 2 < 8:
                    lo(i + 2)
                if i >= 1:
                    ada_mod(i - 1)
                if i >= 2:
                    ada_col(i - 2)
            ada_mod(7)
            ada_col(6)
            ada_col(7)
            dve.wait_ge(s_modcol, 8)
            dve.scalar_tensor_tensor(A1[:, :, :], modcol[:, DC:2 * DC, :], 1.0,
                                     colsT[:, 0:DC].unsqueeze(2).to_broadcast([P, DC, 2]), ALU.add, ALU.mult).then_inc(s_a1, 1)
            for dc in range(DC):
                dve.wait_ge(s_hh, dc + 1)
                dve.tensor_tensor(hTl[:, dc, :], tmp5[:, dc % 4, :], hTh[:, dc, :].bitcast(F32), ALU.subtract).then_inc(s_h, 1)
            for i in range(4):
                first = U_OF[("in", i)]
                base = 8 + 4 * i
                for j in range(4):
                    lo(first + 1 + j)
                    if j == 0 and i >= 2:
                        for b in (2 * i - 4, 2 * i - 3):
                            dve.wait_ge(s_ja, freed(J_OF[("u2", b + 4)])[1])
                            for lo_, n_, x0 in ((U_P, NP, 0), (U_S, NS, NP)):
                                ins = dve.scalar_tensor_tensor(U[:, b, lo_:lo_ + n_], tmp5[:, b % 2, x0:x0 + n_], 1.0,
                                                               U[:, b, lo_:lo_ + n_], ALU.add, ALU.mult)
                            ins.then_inc(s_u, 1)
                    if j >= 1:
                        ada_rows(base + j - 1)
                    if j >= 2:
                        ada_mod(base + j - 2)
                ada_rows(base + 3)
                ada_mod(base + 2)
                ada_mod(base + 3)
            dve.wait_ge(s_u, 4)
            dve.wait_ge(s_lop, lo_count("pool", EARLY))
            dve.wait_ge(s_lov, lo_count("dve", EARLY))
            for i in range(4):
                conv(3)
                n = J_OF[("f", i)]
                dve.wait_ge(s_fh, i + 1)
                for t, b in job_halves(n):
                    ins = dve.tensor_tensor(bl[:, i, t], b, bh[:, i, t].bitcast(F32), ALU.subtract)
                ins.then_inc(s_jd, 1)

            def uv_lo(g):
                for t in range(TT):
                    n = J_OF[("uv", g, t)]
                    dve.wait_ge(s_uvh, TT * g + t + 1)
                    dve.tensor_tensor(uvl[:, g % 2, t, :], bank[n % 2][:, 0:256], uvh[:, g % 2, t, :].bitcast(F32),
                                      ALU.subtract).then_inc(s_jd, 1)

            uv_lo(0)
            for g in range(1, 4):
                uv_lo(g)
                conv(1)
            conv(85)
            for it in range(len(ITEMS) + 2):
                if it < len(ITEMS):
                    blk, h = ITEMS[it]
                    w = it % 2
                    kn = NP if blk < 0 else 384
                    dve.wait_ge(s_sc, it + 1)
                    if it >= 2:
                        dve.wait_ge(s_pt, it - 1)
                    sc = bank[4 + w]
                    if blk < 0:
                        dve.tensor_scalar(sp[:, w, 0:kn], sc[:, 0:kn], SCALE, None, ALU.mult).then_inc(s_ev, 1)
                    else:
                        dve.wait_ge(s_bm, it - 8 + 1)
                        dve.scalar_tensor_tensor(sp[:, w, 0:256], sc[:, 0:256], SCALE,
                                                 bm[:, w].rearrange("p r j -> p (r j)"), ALU.mult, ALU.add)
                        dve.tensor_scalar(sp[:, w, 256:384], sc[:, 256:384], SCALE, None, ALU.mult).then_inc(s_ev, 1)
                    dve.wait_ge(s_ev, it + 1)
                    dve.tensor_reduce(stat[:, 30 + w:31 + w], sp[:, w, 0:kn], AX, ALU.max, negate=True).then_inc(s_mx, 1)
                conv(2)
                if it < len(ITEMS):
                    dve.wait_ge(s_ex, it + 1)
                    link(dve.reciprocal(stat[:, 34 + w:35 + w], stat[:, 32 + w:33 + w]))
                    dve.tensor_scalar(sp[:, w, 0:kn], sp[:, w, 0:kn], stat[:, 34 + w:35 + w], None, ALU.mult).then_inc(s_pn, 1)
                if it >= 2:
                    j = it - 2
                    blk, h = ITEMS[j]
                    r0 = DH * (h % 2)
                    dve.wait_ge(s_pv, j + 1)
                    if blk < 0:
                        dve.tensor_copy(Q[r0:r0 + DH, h // 2, 0:NP], bank[7][r0:r0 + DH, 0:P]).then_inc(s_at, 1)
                    else:
                        dst = Q[r0:r0 + DH, h // 2, NP + P * blk:NP + P * (blk + 1)]
                        dve.tensor_copy(dst, bank[7][r0:r0 + DH, 0:P]).then_inc(s_at, 1)
            conv(len(taps))

            def split_lo(src, n0):
                for c in range(CB):
                    dve.wait_ge(s_bh, n0 + c + 1)
                    dve.tensor_tensor(bl[:, c, :], src(c), bh[:, c, :].bitcast(F32), ALU.subtract).then_inc(s_bl, 1)

            def product(kind, b):
                n = J_OF[(kind, b)]
                dve.wait_ge(s_job, n + 1)
                if b == 0:
                    dve.wait_ge(s_ja, freed(J_OF[({"fnet": "g2", "na": "g1", "conv": "g0"}[kind], 7)])[1])
                dst = M if kind == "fnet" else G
                for t, bk in job_halves(n):
                    ins = dve.scalar_tensor_tensor(dst[:, b, t], G[:, b, t], 1.0, bk, ALU.add, ALU.mult)
                ins.then_inc(s_jd, 1)

            split_lo(lambda c: Z[:, c, :], 0)
            for b in range(DC):
                product("fnet", b)
            dve.wait_ge(s_cv, len(taps))
            for c in range(CB):
                dve.tensor_scalar(Yc[:, c, 0:NP], Y[:, c, 0:NP], 0.5, colsT[:, 8 + c:9 + c], ALU.mult, ALU.add)
                dve.tensor_scalar(Yc[:, c, NP:T], Y[:, c, Y_S:Y_S + NS], 0.5, colsT[:, 8 + c:9 + c], ALU.mult,
                                  ALU.add).then_inc(s_yc, 1)
            dve.wait_ge(s_ln, 1)
            link(dve.tensor_scalar(stat[:, 15:20], bank[7][:, 100:105], -1.0 / 512, None, ALU.mult))
            for t in range(TT):
                ins = dve.tensor_scalar(diag[:, t * P:(t + 1) * P], ident[:, :], stat[:, 15 + t:16 + t], None, ALU.mult)
            ins.then_inc(s_lnd, 1)
            dve.wait_ge(s_ln, 2)
            for c in range(CB):
                dve.tensor_tensor(Yc[:, c, NP:T], Yc[:, c, NP:T], bank[4][:, :], ALU.add)
                dve.tensor_tensor(Yc[:, c, 0:NP], Yc[:, c, 0:NP], bank[5][:, 0:P], ALU.add).then_inc(s_lnc, 1)
            dve.wait_ge(s_ln, 3)
            dve.tensor_scalar(stat[:, 20:25], bank[7][:, 110:115], 1.0 / 512, EPS, ALU.mult, ALU.add).then_inc(s_lns, 1)
            dve.wait_ge(s_lnr, 1)
            for t in range(TT):
                ins = dve.tensor_scalar(diag[:, t * P:(t + 1) * P], ident[:, :], stat[:, 25 + t:26 + t], None, ALU.mult)
            ins.then_inc(s_lnd, 1)
            dve.wait_ge(s_ln, 4)
            for c in range(CB):
                dve.tensor_tensor(Yc[:, c, NP:T], Yc[:, c, NP:T], bank[4][:, :], ALU.mult)
                dve.tensor_tensor(Yc[:, c, 0:NP], Yc[:, c, 0:NP], bank[5][:, 0:P], ALU.mult).then_inc(s_yr, 1)
            for c in range(CB):
                dve.wait_ge(s_bh, CB + c + 1)
                dve.tensor_tensor(bl[:, c, 0:NP], Q[:, c, 0:NP], bh[:, c, 0:NP].bitcast(F32), ALU.subtract)
                tok = "p (r n i) -> p r n i"
                dve.tensor_tensor(bl[:, c, NP:T].rearrange(tok, r=ROWS, n=4), by_block(Q[:, c, NP:T]),
                                  bh[:, c, NP:T].rearrange(tok, r=ROWS, n=4).bitcast(F32), ALU.subtract).then_inc(s_bl, 1)
            for c in range(CB):
                dve.wait_ge(s_yt, c + 1)
                dve.scalar_tensor_tensor(Yc[:, c, :], Yq[:, c, :], 1.0, Yc[:, c, :], ALU.add, ALU.mult).then_inc(s_yz, 1)
            n0 = freed(J_OF[("fnet", 7)])[1]
            for b in range(DC):
                product("na", b)
                dve.wait_ge(s_jd, n0 + b + 1)
                dve.tensor_tensor(M[:, b, :], M[:, b, :], G[:, b, :], ALU.add).then_inc(s_gm, 1)
            dve.wait_ge(s_yz, CB)
            split_lo(lambda c: Yc[:, c, :], 2 * CB)
            n0 = freed(J_OF[("na", 7)])[1]
            for b in range(DC):
                product("conv", b)
                dve.wait_ge(s_jd, n0 + b + 1)
                dve.scalar_tensor_tensor(M[:, b, :], G[:, b, :], 0.5, M[:, b, :], ALU.mult, ALU.add).then_inc(s_gm, 1)
                if b >= 1:
                    dve.wait_ge(s_hh, DC + b)
                    dve.tensor_tensor(hTl[:, b - 1, :], M[:, b - 1, :], hTh[:, b - 1, :].bitcast(F32), ALU.subtract).then_inc(s_h, 1)
            dve.wait_ge(s_hh, 2 * DC)
            dve.tensor_tensor(hTl[:, DC - 1, :], M[:, DC - 1, :], hTh[:, DC - 1, :].bitcast(F32), ALU.subtract).then_inc(s_h, 1)

            def residual(i, t):
                n = J_OF[("out", i, t)]
                g = 0 if t == 0 else 1
                cols = slice(256 * i, 256 * i + 256)
                dve.wait_ge(s_job, n + 1)
                dve.scalar_tensor_tensor(otmp[:, n % 2, :], bank[n % 2][:, 0:256], 0.5, g1bc[:, g, cols], ALU.mult,
                                         ALU.mult).then_inc(s_jd, 1)
                dve.wait_ge(s_jd, freed(n)[1])
                ins = dve.tensor_tensor(X2[:, t, cols], X2[:, t, cols], otmp[:, n % 2, :], ALU.add)
                ins.then_inc(s_x2 if i == 3 else s_xp, 1)

            def norm2(i):
                t = TILE_ORDER[i]
                g = 0 if t == 0 else 1
                dve.wait_ge(s_r2, i + 1)
                if i >= 2:
                    dve.wait_ge(s_hst[i % 2], 16 * (i // 2))
                    dve.wait_ge(s_t2, 2 * i - 2)
                link(dve.scalar_tensor_tensor(h2t[:, i % 2, :], X2[:, t, :], stat[:, 10 + t:11 + t], A2bc[:, g, :],
                                              ALU.mult, ALU.mult))
                dve.tensor_tensor(h2t[:, i % 2, :], h2t[:, i % 2, :], sh2bc[:, g, :], ALU.add).then_inc(s_h2, 1)

            def softmax(i):
                t = TILE_ORDER[i]
                dve.wait_ge(s_lg, i + 1)
                dve.tensor_copy(lgs[:, i, :], bank[7][:, 0:E_N]).then_inc(s_lgc, 1)
                dve.wait_ge(s_lgc, i + 1)
                dve.tensor_reduce(stat[:, 36 + i:37 + i], lgs[:, i, :], AX, ALU.max,
                                  negate=True).then_inc(s_mx2, 1)
                dve.wait_ge(s_ex2, i + 1)
                link(dve.reciprocal(stat[:, 46 + i:47 + i], stat[:, 41 + i:42 + i]))
                dve.tensor_scalar(aff[:, t, :], aff[:, t, :], stat[:, 46 + i:47 + i], None, ALU.mult).then_inc(s_aff, 1)

            dve.wait_ge(s_bc, 16 * 5)
            dve.wait_ge(s_xr, 16 * 5)
            for i in range(3):
                for t in TILE_ORDER:
                    residual(i, t)
            dve.wait_ge(s_bc2, 16 * 4)
            for g in range(2):
                dve.scalar_tensor_tensor(A2bc[:, g, :], A2bc[:, g, :], 1.0, n2bc, ALU.add, ALU.mult).then_inc(s_a2, 1)
            dve.wait_ge(s_a2, 2)
            for m in range(TT + 1):
                if m < TT:
                    residual(3, TILE_ORDER[m])
                if m >= 1:
                    norm2(m - 1)
                if m >= 3:
                    softmax(m - 3)
            softmax(TT - 2)

            def top(x0, x1, v0, cap):
                for r in range(cap // 8):
                    v = slice(v0 + 8 * r, v0 + 8 * r + 8)
                    link(dve.max(vals[:, v], affT[:, x0:x1]))
                    link(dve.max_index(idxu[:, v], vals[:, v], affT[:, x0:x1]))
                    link(dve.match_replace(affT[:, x0:x1], vals[:, v], affT[:, x0:x1], -1.0))

            dve.wait_ge(s_affp, TT - 1)
            link(dve.tensor_copy(affT[:, NP:T], bank[6][0:E_N, :]))
            top(NP, T, 0, CAP_S)
            softmax(TT - 1)
            dve.wait_ge(s_affp, TT)
            link(dve.tensor_copy(affT[:, 0:NP], bank[3][0:E_N, 0:P]))
            top(0, NP, CAP_S, CAP_P)
            dve.tensor_scalar(idxf[:, 0:CAP_S], idxu[:, 0:CAP_S], float(NP), None, ALU.add)
            dve.tensor_copy(idxf[:, CAP_S:M_E], idxu[:, CAP_S:M_E]).then_inc(s_idx, 1)
            dve.wait_ge(s_idxp, 1)
            dve.tensor_copy(idxT[:, :], bank[4][0:M_E, 0:E_N]).then_inc(s_route, 1)
            dve.tensor_copy(gateT[:, :], bank[4][0:M_E, E_N:2 * E_N]).then_inc(s_route, 1)
            dve.wait_ge(s_route, 2)
            dve.wait_ge(s_g2, 32)

            def e_lo_unit(e, k):
                dve.wait_ge(e_hi, 12 * e + (k + 1))
                dve.tensor_tensor(l2r[:, k % 3, :], w2[:, k, :], h2r[:, k % 3, :].bitcast(F32),
                                  ALU.subtract).then_inc(e_lo, 1)

            def x_lo(e):
                for hf in range(2):
                    dve.wait_ge(e_xh, 2 * e + (hf + 1))
                    dve.tensor_tensor(xTl[:, 4 * hf:4 * hf + 4, :], bank[6 + hf][:, 0:4 * M_E].rearrange("p (c t) -> p c t", c=4),
                                      xTh[:, 4 * hf:4 * hf + 4, :].bitcast(F32), ALU.subtract).then_inc(e_xl, 1)

            def gated(e, hf):
                dve.wait_ge(e_unit, 12 * e + (4 * hf + 4))
                dve.wait_ge(e_sg, 2 * e + (hf + 1))
                x = sg[:, 512 * hf:512 * hf + 512]
                dve.tensor_tensor(x, x, bank[2 + hf][0:M_E, :], ALU.mult).then_inc(e_h, 1)

            def h_lo(e, hf):
                dve.wait_ge(e_hh, 2 * e + (hf + 1))
                dve.tensor_tensor(hTl2[:, 4 * hf:4 * hf + 4, :], bank[hf][:, 0:4 * M_E].rearrange("p (c t) -> p c t", c=4),
                                  hTh2[:, 4 * hf:4 * hf + 4, :].bitcast(F32), ALU.subtract).then_inc(e_hl, 1)

            def expert(e, last):
                e_lo_unit(e, 4)
                e_lo_unit(e, 5)
                gated(e, 0)
                e_lo_unit(e, 6)
                e_lo_unit(e, 7)
                h_lo(e, 0)
                e_lo_unit(e, 8)
                e_lo_unit(e, 9)
                gated(e, 1)
                e_lo_unit(e, 10)
                h_lo(e, 1)
                e_lo_unit(e, 11)
                if not last:
                    e_lo_unit(e + 1, 0)
                    x_lo(e + 1)
                    e_lo_unit(e + 1, 1)
                    e_lo_unit(e + 1, 2)
                dve.wait_ge(e_unit, 12 * e + 12)
                if not (isinstance(e, int) and e == 0):
                    dve.wait_ge(e_add, 16 * e)
                for hf in range(2):
                    x = slice(512 * hf, 512 * hf + 512)
                    dve.scalar_tensor_tensor(ye[:, x], bank[4 + hf][0:M_E, :], gateT[:, at(e)], g2r[:, x], ALU.mult,
                                             ALU.mult).then_inc(e_y, 1)
                if not last:
                    e_lo_unit(e + 1, 3)

            x_lo(0)
            dve.wait_ge(e_lo, 3)
            e_lo_unit(0, 3)
            expert(0, False)
            with dve.Fori(1, E_N - 1) as e:
                expert(e, False)
            expert(E_N - 1, True)
            dve.wait_ge(s_fg, 16)
            for t in range(TT):
                dve.wait_ge(s_fr, t + 1)
                dve.scalar_tensor_tensor(fin[:, t, :], fin[:, t, :], stat[:, 10 + t:11 + t], fgbc, ALU.mult,
                                         ALU.mult).then_inc(s_fy, 1)

        @block.tensor
        def _(pe):
            def mm3(out, lh, ll, rh, rl, start, stop):
                pe.matmul(out, lh, rh, start=start, stop=False)
                pe.matmul(out, lh, rl, start=False, stop=False)
                return pe.matmul(out, ll, rh, start=False, stop=stop)

            def bank_free(n):
                if n >= 2:
                    dve, count = freed(n - 2)
                    pe.wait_ge(s_jd if dve else s_ja, count)

            def slot(u):
                return unit_view(split(u)[0], u), unit_view(split(u)[1], u)

            def block_steps(n, u, c0, xh, xl, nk, wait_h=False):
                wh, wl = slot(u)
                (t0, b0), (t1, b1) = job_halves(n)
                for c in range(nk):
                    if c == 0:
                        bank_free(n)
                    if wait_h:
                        pe.wait_ge(s_h, c + 1)
                    a_h, a_l = wh[:, c, c0:c0 + P], wl[:, c, c0:c0 + P]
                    st, en = c == 0, c == nk - 1
                    pe.matmul(b0, a_h, xh[:, c, t0], start=st, stop=False)
                    pe.matmul(b1, a_h, xh[:, c, t1], start=st, stop=False)
                    pe.matmul(b0, a_h, xl[:, c, t0], start=False, stop=False)
                    pe.matmul(b1, a_h, xl[:, c, t1], start=False, stop=False)
                    pe.matmul(b0, a_l, xh[:, c, t0], start=False, stop=en)
                    last = pe.matmul(b1, a_l, xh[:, c, t1], start=False, stop=en)
                    if en:
                        last.then_inc(s_job, 1)
                    yield last

            def run(steps):
                for _ in steps:
                    pass

            def in_block(kind, b):
                u = U_OF[("in", {"u2": 0, "q": 4, "k": 6, "f": 10, "g0": 12, "g1": 16, "g2": 20}[kind] + b // 2)]
                return block_steps(J_OF[(kind, b)], u, P * (b % 2), hTh, hTl, DC, (kind, b) == ("u2", 0)), u

            pe.wait_ge(s_cst, 16 * N_CST)
            for dc in range(DC):
                pe.transpose(bank[7][:, 2 * dc:2 * dc + 2], c2[:, dc * P:(dc + 1) * P], ident[0:2, 0:2])
            pe.transpose(bank[7][:, 16:36], rows20, ident[0:20, 0:20])
            for c in range(CB):
                pe.transpose(bank[7][:, 64 + CW * c:64 + CW * (c + 1)], cwr[:, c * P:(c + 1) * P], ident[0:CW, 0:CW])
            for c in range(CB):
                last = pe.transpose(bank[6][:, c * P:(c + 1) * P], kraw[:, c * P:(c + 1) * P], ident[:, :])
            last.then_inc(s_turn, 1)

            def ada(i):
                u = U_OF[("ada", i)]
                lo_ready(pe, u)
                if i >= 2:
                    pe.wait_ge(s_rows4, i - 1)
                wh, wl = slot(u)
                for dc in range(DC):
                    pe.matmul(bank[4 + i % 2][:, 0:256], c4[:, dc, :], wh[:, dc, :], start=dc == 0, stop=False)
                    last = pe.matmul(bank[4 + i % 2][:, 0:256], c4[:, dc, :], wl[:, dc, :], start=False, stop=dc == DC - 1)
                last.then_inc(s_ada, 1)

            def ada_sum(i):
                pe.wait_ge(s_rows4, i + 1)
                if i >= 1:
                    pe.wait_ge(s_modrow, i)
                pe.matmul(bank[7][0:2, 256:512], sel4[:, :], rows4[:, i % 2, :], start=True, stop=False)
                pe.matmul(bank[7][0:2, 256:512], pick24[:, i, :], bias24, start=False,
                          stop=True).then_inc(s_mrow, 1)

            def ada_turn(i):
                pe.wait_ge(s_modrow, i + 1)
                if i >= 1:
                    pe.wait_ge(s_modcol, i)
                for j in range(2):
                    last = pe.transpose(bank[6][:, 2 * j:2 * j + 2], modrow[:, i % 2, j * P:(j + 1) * P], ident[0:2, 0:2])
                last.then_inc(s_mcol, 1)

            pe.wait_ge(s_cast, 2)
            pe.wait_ge(s_turned, 1)
            for i in range(8):
                ada(i)
                if i >= 1:
                    ada_sum(i - 1)
                if i >= 2:
                    ada_turn(i - 2)
            ada_sum(7)
            ada_turn(6)
            ada_turn(7)
            pe.wait_ge(s_xhat, TT)
            for dc in range(DC):
                n = J_OF[("xT", dc)]
                bank_free(n)
                bs, bp = job_bank(n)
                for t in range(4):
                    pe.transpose(bs[:, t * P:(t + 1) * P], X[:, 1 + t, dc * P:(dc + 1) * P], ident[:, :])
                pe.transpose(bp, X[:, 0, dc * P:(dc + 1) * P], ident[:, :]).then_inc(s_job, 1)
            pe.wait_ge(s_modcol, 8)
            for i in range(4):
                for b in (2 * i, 2 * i + 1):
                    steps, u = in_block("u2", b)
                    lo_ready(pe, u)
                    run(steps)
                base = 8 + 4 * i
                for j in range(4):
                    ada(base + j)
                    if j >= 1:
                        ada_sum(base + j - 1)
                ada_sum(base + 3)
            for b in range(4):
                steps, u = in_block("f", b)
                lo_ready(pe, u)
                run(steps)

            def uv(g):
                for t in range(TT):
                    n = J_OF[("uv", g, t)]
                    bank_free(n)
                    x = slice(t * P, (t + 1) * P)
                    mm3(bank[n % 2][:, 0:256], bh[:, g, x], bl[:, g, x], gtab_h[:, 0:256], gtab_l[:, 0:256], True,
                        True).then_inc(s_job, 1)

            pe.wait_ge(s_jd, freed(J_OF[("f", 3)])[1])
            pe.wait_ge(s_cast, 4)
            uv(0)
            u = U_OF[("dft", 0)]
            (ch, cl), (sh, sl) = slot(u), slot(u + 1)
            for g in range(4):
                if g < 3:
                    uv(g + 1)
                if g == 0:
                    lo_ready(pe, u + 1)
                n = J_OF[("z", g)]
                pe.wait_ge(s_jd, freed(J_OF[("uv", g, TT - 1)])[1])
                bank_free(n)
                bs, bp = job_bank(n)
                w = g % 2
                for c in range(4):
                    mm3(bs, uvh[:, w, c + 1, 0:P], uvl[:, w, c + 1, 0:P], ch[:, c, :], cl[:, c, :], c == 0, False)
                    mm3(bs, uvh[:, w, c + 1, P:2 * P], uvl[:, w, c + 1, P:2 * P], sh[:, c, :], sl[:, c, :], False, c == 3)
                mm3(bp, uvh[:, w, 0, 0:P], uvl[:, w, 0, 0:P], gtab_h[:, 0:P], gtab_l[:, 0:P], True, False)
                mm3(bp, uvh[:, w, 0, P:2 * P], uvl[:, w, 0, P:2 * P], gtab_h[:, 2 * P:3 * P], gtab_l[:, 2 * P:3 * P],
                    False, True).then_inc(s_job, 1)
            for kind in ("q", "k"):
                for b in range(4):
                    steps, u = in_block(kind, b)
                    lo_ready(pe, u)
                    run(steps)

            def token_major(kind, i, t, u):
                n = J_OF[(kind, i, t)]
                bank_free(n)
                wh, wl = slot(u)
                x = slice(t * P, (t + 1) * P)
                for dc in range(DC):
                    if kind == "out" and i == 0 and t == TILE_ORDER[0]:
                        pe.wait_ge(s_h, DC + dc + 1)
                    last = mm3(bank[n % 2][:, 0:256], hTh[:, dc, x], hTl[:, dc, x], wh[:, dc, :], wl[:, dc, :], dc == 0,
                               dc == DC - 1)
                last.then_inc(s_job, 1)

            for i in range(2):
                u = U_OF[("in", 8 + i)]
                lo_ready(pe, u)
                for t in range(TT):
                    token_major("v", i, t, u)
            pe.wait_ge(s_ja, freed(J_OF[("k", 3)])[1])
            for c in range(4):
                last = pe.transpose(bank[6][:, c * P:(c + 1) * P], K[:, c, 0:NP], ident[:, :])
            last.then_inc(s_kt, 1)

            pe.wait_ge(s_ja, freed(J_OF[("v", 1, 4)])[1])
            pe.wait_ge(s_x, 16 * 6)
            pe.wait_ge(s_ko, 1)
            gate_steps = []
            for b in range(DC):
                steps, u = in_block("g2", b)
                gate_steps.append((steps, u))

            for it in range(len(ITEMS) + 2):
                if it < len(ITEMS):
                    blk, h = ITEMS[it]
                    r = slice(DH * (h % 2), DH * (h % 2) + DH)
                    hc = h // 2
                    sc = bank[4 + it % 2]
                    if it >= 2:
                        pe.wait_ge(s_ev, it - 1)
                    if blk < 0:
                        pe.matmul(sc[:, 0:P], Q[r, hc, 0:NP], K[r, hc, 0:NP], start=True, stop=True).then_inc(s_sc, 1)
                    else:
                        q = Q[r, hc, NP + P * blk:NP + P * (blk + 1)]
                        k = K[r, hc, NP:T].rearrange("p (r c) -> p r c", c=GW)[:, :, KB[blk]:KB[blk] + 32]
                        pe.matmul(sc[:, 0:256], q, k, start=True, stop=True)
                        pe.matmul(sc[:, 256:384], q, kcT[r, hc, :], start=True, stop=True).then_inc(s_sc, 1)
                    for n in range(gate_step(it), gate_step(it + 1)):
                        if n % DC == 0:
                            lo_ready(pe, gate_steps[n // DC][1])
                        next(gate_steps[n // DC][0])
                if 1 <= it <= len(ITEMS):
                    j = it - 1
                    blk = ITEMS[j][0]
                    pe.wait_ge(s_pn, j + 1)
                    if j >= 1:
                        pe.wait_ge(s_pte, j)
                    for c in range(1 if blk < 0 else 3):
                        last = pe.transpose(bank[6][:, c * P:(c + 1) * P], sp[:, j % 2, c * P:(c + 1) * P], ident[:, :])
                    last.then_inc(s_pt, 1)
                if it >= 2:
                    j = it - 2
                    blk, h = ITEMS[j]
                    pe.wait_ge(s_pte, j + 1)
                    if j >= 1:
                        pe.wait_ge(s_at, j)
                    if blk >= 0 and h == 0:
                        pe.wait_ge(s_vw[blk % 2], 32 * (blk // 2 + 1))
                    out = bank[7][DH * (h % 2):DH * (h % 2) + DH, 0:P]
                    cols = slice(DH * h, DH * h + DH)
                    vals_ = [vp[:, cols]] if blk < 0 else [vw[:, blk % 2, 0, cols], vw[:, blk % 2, 1, cols], vc[:, cols]]
                    for c, v in enumerate(vals_):
                        last = pe.matmul(out, v, pT[:, j % 2, c * P:(c + 1) * P], start=c == 0, stop=c == len(vals_) - 1)
                    last.then_inc(s_pv, 1)

            run(gate_steps[DC - 1][0])

            def branch(kind, n_split):
                for b in range(DC):
                    u = U_OF[(kind, b // 4)]
                    if b % 4 == 0:
                        lo_ready(pe, u)
                    if b == 0:
                        pe.wait_ge(s_bl, n_split)
                    run(block_steps(J_OF[(kind, b)], u, P * (b % 4), bh, bl, CB))

            def gate(kind, b):
                steps, u = in_block(kind, b)
                lo_ready(pe, u)
                run(steps)

            def ln_sums(src, col):
                for t in range(TT):
                    for c in range(CB):
                        last = pe.matmul(bank[7][:, col + t:col + t + 1], src[:, c, t * P:(t + 1) * P], ones[:, 0:1],
                                         start=c == 0, stop=c == CB - 1)
                last.then_inc(s_ln, 1)

            def ln_spread(n):
                pe.wait_ge(s_lnd, n)
                pe.matmul(bank[4][:, :], ones[:, :], diag[:, NP:T], start=True, stop=True)
                pe.matmul(bank[5][:, 0:P], ones[:, :], diag[:, 0:NP], start=True, stop=True).then_inc(s_ln, 1)

            branch("fnet", CB)
            for b in range(DC):
                gate("g1", b)
                if b == 0:
                    pe.wait_ge(s_yc, CB)
                    ln_sums(Yc, 100)
                if b == 1:
                    ln_spread(1)
                if b == 3:
                    pe.wait_ge(s_ysq, CB)
                    ln_sums(Yq, 110)
                if b == 5:
                    ln_spread(2)
            branch("na", 2 * CB)
            for b in range(DC):
                gate("g0", b)
            branch("conv", 3 * CB)
            for i in range(3):
                u = U_OF[("out", i)]
                lo_ready(pe, u)
                for t in TILE_ORDER:
                    token_major("out", i, t, u)

            def turn2(i):
                pe.wait_ge(s_h2, i + 1)
                if i >= 1:
                    pe.wait_ge(s_t2e, 2 * i)
                for hf in range(2):
                    for c in range(4):
                        dc = 4 * hf + c
                        last = pe.transpose(bank[4 + hf][:, c * P:(c + 1) * P], h2t[:, i % 2, dc * P:(dc + 1) * P], ident[:, :])
                    last.then_inc(s_t2, 1)

            def route(i):
                pe.wait_ge(s_t2e, 2 * i + 2)
                pe.wait_ge(s_bc2, 16 * 4)
                if i >= 1:
                    pe.wait_ge(s_lgc, i)
                out = bank[7][:, 0:E_N]
                for dc in range(DC):
                    pe.matmul(out, h2T[:, i % 2, dc, :], wr[:, dc, :], start=dc == 0, stop=False)
                pe.matmul(out, ones[0:1, :], br, start=False, stop=True).then_inc(s_lg, 1)

            def turn_aff(i):
                t = TILE_ORDER[i]
                pe.wait_ge(s_aff, i + 1)
                dst = bank[3][0:E_N, 0:P] if t == 0 else bank[6][0:E_N, (t - 1) * P:t * P]
                pe.transpose(dst, aff[:, t, :], ident[:, :]).then_inc(s_affp, 1)

            u = U_OF[("out", 3)]
            lo_ready(pe, u)
            for m in range(TT + 2):
                if m < TT:
                    token_major("out", 3, TILE_ORDER[m], u)
                if m >= 2:
                    turn2(m - 2)
                    route(m - 2)
                if m >= TT:
                    turn_aff(m - TT)
            for i in range(2, TT):
                turn_aff(i)
            pe.wait_ge(s_idx, 1)
            pe.transpose(bank[4][0:M_E, 0:E_N], idxf, ident[0:E_N, 0:E_N])
            pe.transpose(bank[4][0:M_E, E_N:2 * E_N], vals, ident[0:E_N, 0:E_N]).then_inc(s_idxp, 1)

            def turn_tokens(e):
                pe.wait_ge(e_x, 16 * e + 16)
                for hf in range(2):
                    for c in range(4):
                        dc = 4 * hf + c
                        last = pe.transpose(bank[6 + hf][:, c * M_E:(c + 1) * M_E], xe[:, dc * P:(dc + 1) * P],
                                            ident[0:M_E, 0:M_E])
                    last.then_inc(e_xt, 1)

            def gate_up(e, k):
                name, ch, r = EXPERT_UNITS[k]
                pe.wait_ge(e_lo, 12 * e + (k + 1))
                wh = h2r[:, k % 3, :].rearrange("p (c n) -> p c n", c=4)
                wl = l2r[:, k % 3, :].rearrange("p (c n) -> p c n", c=4)
                out = bank[(0 if name == "w_e_gate" else 2) + ch][0:M_E, :]
                for c in range(4):
                    last = mm3(out, xTh[:, 4 * r + c, :], xTl[:, 4 * r + c, :], wh[:, c, :], wl[:, c, :],
                               r == 0 and c == 0, r == 1 and c == 3)
                last.then_inc(e_unit, 1)

            def down(e, k):
                pe.wait_ge(e_lo, 12 * e + (k + 1))
                wh = h2r[:, k % 3, :].rearrange("p (c n) -> p c n", c=2)
                wl = l2r[:, k % 3, :].rearrange("p (c n) -> p c n", c=2)
                q = k - 8
                for c in range(2):
                    for hf in range(2):
                        n = slice(512 * hf, 512 * hf + 512)
                        last = mm3(bank[4 + hf][0:M_E, :], hTh2[:, 2 * q + c, :], hTl2[:, 2 * q + c, :], wh[:, c, n],
                                   wl[:, c, n], q == 0 and c == 0, q == 3 and c == 1)
                last.then_inc(e_unit, 1)

            def turn_h(e, hf):
                pe.wait_ge(e_h, 2 * e + (hf + 1))
                for c in range(4):
                    fc = 4 * hf + c
                    ins = pe.transpose(bank[hf][:, c * M_E:(c + 1) * M_E], sg[:, fc * P:(fc + 1) * P], ident[0:M_E, 0:M_E])
                ins.then_inc(e_ht, 1)

            def expert(e, last):
                pe.wait_ge(e_xl, 2 * e + 2)
                for k in range(5):
                    gate_up(e, k)
                turn_h(e, 0)
                for k in range(5, 8):
                    gate_up(e, k)
                if not (isinstance(e, int) and e == 0):
                    pe.wait_ge(e_y, 2 * e)
                pe.wait_ge(e_hl, 2 * e + 1)
                down(e, 8)
                turn_h(e, 1)
                down(e, 9)
                if not last:
                    turn_tokens(e + 1)
                pe.wait_ge(e_hl, 2 * e + 2)
                down(e, 10)
                down(e, 11)

            turn_tokens(0)
            expert(0, False)
            with pe.Fori(1, E_N - 1) as e:
                expert(e, False)
            expert(E_N - 1, True)


_INS = ["x_prompt", "x_sample", "cache_k", "cache_v", "c", "c_ctx", "w_ada", "b_ada", "norm1_g", "w_in", "conv_w", "conv_b",
        "conv_ln_g", "conv_ln_b", "w_conv_out", "rpb", "w_na_out", "w_fnet", "w_out", "norm2_g", "w_router", "b_router",
        "w_e_gate", "w_e_up", "w_e_down", "final_norm_g"]
_OUTS = [(1, NP, D), (1, NS, D), (1, 1, NP, H, DH), (1, 1, NP, H, DH)]
_SCRATCH = [("mods", (2, 4 * D)), ("rpbpad", (16, RPL)), ("vals", (NS, 512)), ("h2", (T, D)), ("acc", (T, D))]


def shape_constants():
    p = np.arange(P)
    ang = 2 * np.pi * np.outer(p, p) / P
    dft_g = np.concatenate([np.cos(ang), -np.sin(ang), np.sin(ang)], axis=1) / np.sqrt(P)
    ll, kk = np.arange(NS), np.arange(NS)
    ang = 2 * np.pi * (np.outer(ll, kk) % NS) / NS
    dft_l = np.stack([np.cos(ang), np.sin(ang)]) / np.sqrt(NS)
    dft_l = dft_l.reshape(2, 4, P, NS).transpose(0, 2, 1, 3)
    i, j = np.arange(16)[:, None], np.arange(32)[None, :]
    mask = []
    for blk in (0, 1, 3):
        col, key = 16 * blk + i, KB[blk] + j
        start = np.clip(col - 8, 0, GW - 16)
        mask.append(np.where((key >= start) & (key < start + 16), 0.0, -1e30))
    mask = np.tile(np.stack(mask, axis=1), (8, 1, 1))
    sel4 = np.array([[1, 0], [0, 1], [1, 0], [0, 1]])
    pick = np.repeat(np.eye(24)[:, :, None], 2, axis=2)
    made = {"pick": pick, "ident": np.eye(P), "ones": np.ones((P, P)), "dft_g": dft_g, "dft_l": dft_l, "mask": mask, "sel4": sel4}
    return {k: np.ascontiguousarray(v, dtype=np.float32) for k, v in made.items()}


def kernel(**inputs):
    import concourse.bacc as _bacc
    from concourse.bass_utils import run_bass_kernel_spmd as _run

    nc = _bacc.Bacc("TRN2", target_bir_lowering=False, num_devices=1)
    arrays, a = {}, {}
    for name in _INS:
        x = np.ascontiguousarray(inputs[name])
        arrays["in_" + name] = x
        a[name] = nc.dram_tensor("in_" + name, x.shape, F32, kind="ExternalInput").ap()
    consts = {}
    for name, x in shape_constants().items():
        arrays["const_" + name] = x
        consts[name] = nc.dram_tensor("const_" + name, x.shape, F32, kind="ExternalInput").ap()
    outs = [nc.dram_tensor(f"out_{i}", s, F32, kind="ExternalOutput").ap() for i, s in enumerate(_OUTS)]
    scratch = [nc.dram_tensor("scratch_" + n, s, F32, kind="Internal").ap() for n, s in _SCRATCH]
    trunk(nc, a, outs, consts, scratch)
    r = _run(nc, [arrays], core_ids=[0])
    return tuple(r.results[0][f"out_{i}"] for i in range(len(_OUTS)))
```
